# Optimizing a Trainium2 kernel written in Bass

```python
import jax
import jax.numpy as jnp
from jax import lax
import numpy as np

D_MODEL = 1024
BATCH = 1
SEQ = 1024
DEPTH = 2

N_MEM = 256
EPS = 1e-6
CHUNK = 64
CONV_W = 4
GLA_HEADS = 4
GLA_DK = 64
GLA_DV = 128
GLA_KEY = GLA_HEADS * GLA_DK
GLA_VAL = GLA_HEADS * GLA_DV
GLA_GATE_RANK = 16
GLA_GATE_NORM = 16.0
LRU_WIDTH = D_MODEL // 2
LRU_BLOCKS = 4
LRU_BLOCK = LRU_WIDTH // LRU_BLOCKS
LRU_C = 8.0
AB_IN = 2 * GLA_KEY + 2 * GLA_VAL + GLA_GATE_RANK + 2 * LRU_WIDTH
AB_MIX = GLA_VAL + LRU_WIDTH
GDN_HEADS = 8
GDN_DK = 128
GDN_DV = 128
GDN_KEY = GDN_HEADS * GDN_DK
GDN_VAL = GDN_HEADS * GDN_DV
GDN_CONV_CH = 2 * GDN_KEY + GDN_VAL
GDN_IN = GDN_CONV_CH + GDN_VAL + 2 * GDN_HEADS
XA_HEADS = 4
XA_DH = D_MODEL // XA_HEADS
D_FF = 4 * D_MODEL
N_EVEN = (DEPTH + 1) // 2
N_ODD = DEPTH // 2

kernel_name = "hybrid_gla_rglru_gdn_memxattn_block"

F32 = jnp.float32

def rms_norm(x, g):
    xf = x.astype(F32)
    y = xf * lax.rsqrt(jnp.mean(xf * xf, axis=-1, keepdims=True) + EPS)
    return (y * g.astype(F32)).astype(x.dtype)

def l2_norm(x):
    xf = x.astype(F32)
    return xf * lax.rsqrt(jnp.sum(xf * xf, axis=-1, keepdims=True) + EPS)

def causal_dwconv(x, w, b=None):
    K = w.shape[0]
    T = x.shape[1]
    xp = jnp.pad(x, ((0, 0), (K - 1, 0), (0, 0)))
    y = xp[:, 0:T] * w[0]
    for kk in range(1, K):
        y = y + xp[:, kk:kk + T] * w[kk]
    if b is not None:
        y = y + b
    return y

def gla_chunked(q, k, v, gk):
    B, T, H, dk = q.shape
    dv = v.shape[-1]
    N = T // CHUNK

    def to_chunks(t):
        return t.astype(F32).reshape(B, N, CHUNK, H, t.shape[-1]).transpose(1, 0, 3, 2, 4)

    qc_all = to_chunks(q) * (dk ** -0.5)
    kc_all = to_chunks(k)
    vc_all = to_chunks(v)
    bc_all = jnp.cumsum(to_chunks(gk), axis=-2)
    causal = jnp.tril(jnp.ones((CHUNK, CHUNK), dtype=bool))

    def step(S, inp):
        qc, kc, vc, bc = inp
        diff = bc[..., :, None, :] - bc[..., None, :, :]
        decay = jnp.exp(jnp.where(causal[:, :, None], diff, -jnp.inf))
        A = jnp.einsum('bhid,bhijd,bhjd->bhij', qc, decay, kc)
        o = jnp.einsum('bhij,bhjv->bhiv', A, vc) + jnp.einsum('bhid,bhdv->bhiv', qc * jnp.exp(bc), S)
        blast = bc[..., -1:, :]
        S = S * jnp.exp(blast[..., 0, :])[..., None] + jnp.einsum('bhjd,bhjv->bhdv', kc * jnp.exp(blast - bc), vc)
        return S, o

    S0 = jnp.zeros((B, H, dk, dv), F32)
    _, o = lax.scan(step, S0, (qc_all, kc_all, vc_all, bc_all))
    return o.transpose(1, 0, 3, 2, 4).reshape(B, T, H, dv)

def rglru(x, w_a, b_a, w_x, b_x, lam):
    B, T, W = x.shape
    xf = x.astype(F32)
    xb = xf.reshape(B, T, LRU_BLOCKS, LRU_BLOCK)
    r = jax.nn.sigmoid(jnp.einsum('btni,nij->btnj', xb, w_a.astype(F32)).reshape(B, T, W) + b_a.astype(F32))
    i_g = jax.nn.sigmoid(jnp.einsum('btni,nij->btnj', xb, w_x.astype(F32)).reshape(B, T, W) + b_x.astype(F32))
    log_a = -LRU_C * r * jax.nn.softplus(-lam.astype(F32))
    a = jnp.exp(log_a)
    u = jnp.sqrt(-jnp.expm1(2.0 * log_a)) * (i_g * xf)

    def combine(left, right):
        return (left[0] * right[0], right[0] * left[1] + right[1])

    _, h = lax.associative_scan(combine, (a, u), axis=1)
    return h

def gated_delta_chunked(q, k, v, g, beta):
    B, T, H, dk = q.shape
    dv = v.shape[-1]
    N = T // CHUNK

    def to_chunks(t):
        return t.astype(F32).reshape(B, N, CHUNK, H, t.shape[-1]).transpose(0, 3, 1, 2, 4)

    qc = to_chunks(q) * (dk ** -0.5)
    kc = to_chunks(k)
    vc = to_chunks(v)
    gcum = jnp.cumsum(g.astype(F32).reshape(B, N, CHUNK, H).transpose(0, 3, 1, 2), axis=-1)
    bt = beta.astype(F32).reshape(B, N, CHUNK, H).transpose(0, 3, 1, 2)[..., None]
    incl = jnp.tril(jnp.ones((CHUNK, CHUNK), dtype=bool))
    strict = jnp.tril(jnp.ones((CHUNK, CHUNK), dtype=bool), k=-1)
    L = jnp.exp(jnp.where(incl, gcum[..., :, None] - gcum[..., None, :], -jnp.inf))
    kb = kc * bt
    vb = vc * bt
    M = jnp.where(strict, jnp.einsum('bhnid,bhnjd->bhnij', kb, kc) * L, 0.0)
    IM = M + jnp.eye(CHUNK, dtype=F32)
    rhs = jnp.concatenate([vb, kb * jnp.exp(gcum)[..., None]], axis=-1)
    sol = lax.linalg.triangular_solve(IM, rhs, left_side=True, lower=True, unit_diagonal=True)
    u_all = sol[..., :dv]
    w_all = sol[..., dv:]
    Aqk = jnp.where(incl, jnp.einsum('bhnid,bhnjd->bhnij', qc, kc) * L, 0.0)

    def nfirst(t):
        return jnp.moveaxis(t, 2, 0)

    def step(S, inp):
        qn, kn, un, wn, an, gn = inp
        v_new = un - jnp.einsum('bhcd,bhdv->bhcv', wn, S)
        o = jnp.einsum('bhcd,bhdv->bhcv', qn * jnp.exp(gn)[..., None], S) + jnp.einsum('bhij,bhjv->bhiv', an, v_new)
        glast = gn[..., -1]
        S = S * jnp.exp(glast)[..., None, None] + jnp.einsum('bhcd,bhcv->bhdv', kn * jnp.exp(glast[..., None] - gn)[..., None], v_new)
        return S, o

    S0 = jnp.zeros((B, H, dk, dv), F32)
    _, o = lax.scan(step, S0, (nfirst(qc), nfirst(kc), nfirst(u_all), nfirst(w_all), nfirst(Aqk), nfirst(gcum)))
    return o.transpose(1, 0, 3, 2, 4).reshape(B, T, H, dv)

def gla_lru_mixer(h, w_in, gk_w2, gk_b, gla_g, conv_w, conv_b, w_a, b_a, w_x, b_x, lam, w_out):
    B, T, _ = h.shape
    proj = h @ w_in
    o1 = GLA_KEY
    o2 = o1 + GLA_KEY
    o3 = o2 + GLA_VAL
    o4 = o3 + GLA_VAL
    o5 = o4 + GLA_GATE_RANK
    o6 = o5 + LRU_WIDTH
    q, k, v, g_out, gk_lr, lru_x, lru_gate = jnp.split(proj, [o1, o2, o3, o4, o5, o6], axis=-1)
    gk = jax.nn.log_sigmoid((gk_lr @ gk_w2 + gk_b).astype(F32)) / GLA_GATE_NORM
    o = gla_chunked(q.reshape(B, T, GLA_HEADS, GLA_DK), k.reshape(B, T, GLA_HEADS, GLA_DK),
                    v.reshape(B, T, GLA_HEADS, GLA_DV), gk.reshape(B, T, GLA_HEADS, GLA_DK))
    o = rms_norm(o, gla_g) * jax.nn.silu(g_out.reshape(B, T, GLA_HEADS, GLA_DV).astype(F32))
    xr = causal_dwconv(lru_x, conv_w, conv_b)
    y = rglru(xr, w_a, b_a, w_x, b_x, lam) * jax.nn.gelu(lru_gate.astype(F32))
    mixed = jnp.concatenate([o.reshape(B, T, GLA_VAL), y], axis=-1).astype(h.dtype)
    return mixed @ w_out

def gdn_mixer(h, w_in, conv_w, a_log, dt_bias, norm_g, w_out):
    B, T, _ = h.shape
    proj = h @ w_in
    p1 = GDN_CONV_CH
    p2 = p1 + GDN_VAL
    p3 = p2 + GDN_HEADS
    qkv, z, b_logit, a_logit = jnp.split(proj, [p1, p2, p3], axis=-1)
    qkv = jax.nn.silu(causal_dwconv(qkv, conv_w))
    q, k, v = jnp.split(qkv, [GDN_KEY, 2 * GDN_KEY], axis=-1)
    q = l2_norm(q.reshape(B, T, GDN_HEADS, GDN_DK))
    k = l2_norm(k.reshape(B, T, GDN_HEADS, GDN_DK))
    beta = jax.nn.sigmoid(b_logit.astype(F32))
    g = -jnp.exp(a_log.astype(F32)) * jax.nn.softplus(a_logit.astype(F32) + dt_bias.astype(F32))
    o = gated_delta_chunked(q, k, v.reshape(B, T, GDN_HEADS, GDN_DV), g, beta)
    o = rms_norm(o, norm_g) * jax.nn.silu(z.reshape(B, T, GDN_HEADS, GDN_DV).astype(F32))
    return o.reshape(B, T, GDN_VAL).astype(h.dtype) @ w_out

def mem_cross_attn(h, mem_n, w_q, w_kv, w_o):
    B, T, _ = h.shape
    M = mem_n.shape[1]
    q = (h @ w_q).reshape(B, T, XA_HEADS, XA_DH).astype(F32)
    kv = mem_n @ w_kv
    k = kv[..., :D_MODEL].reshape(B, M, XA_HEADS, XA_DH).astype(F32)
    v = kv[..., D_MODEL:].reshape(B, M, XA_HEADS, XA_DH).astype(F32)
    s = jnp.einsum('bthd,bmhd->bhtm', q, k) * (XA_DH ** -0.5)
    p = jax.nn.softmax(s, axis=-1)
    o = jnp.einsum('bhtm,bmhd->bthd', p, v).reshape(B, T, D_MODEL).astype(h.dtype)
    return o @ w_o

def sq_relu_mlp(h, w1, w2):
    return jnp.square(jax.nn.relu(h @ w1)) @ w2

def setup_inputs(seed: int = 0) -> dict:
    key = jax.random.key(seed)
    ks = iter(jax.random.split(key, 64))

    def nrm(shape, fan_in):
        return jax.random.normal(next(ks), shape, F32) * (fan_in ** -0.5)

    def gain(shape):
        return 1.0 + 0.02 * jax.random.normal(next(ks), shape, F32)

    def small(shape):
        return 0.01 * jax.random.normal(next(ks), shape, F32)

    x = jax.random.normal(next(ks), (BATCH, SEQ, D_MODEL), F32)
    mem = jax.random.normal(next(ks), (BATCH, N_MEM, D_MODEL), F32)
    u = jax.random.uniform(next(ks), (N_EVEN, LRU_WIDTH), F32, minval=0.9, maxval=0.999)
    p = u ** (1.0 / LRU_C)
    lru_lambda = jnp.log(p) - jnp.log1p(-p)
    gdn_a_log = jnp.log(jax.random.uniform(next(ks), (N_ODD, GDN_HEADS), F32, minval=1.0, maxval=16.0))
    dt = jnp.exp(jax.random.uniform(next(ks), (N_ODD, GDN_HEADS), F32, minval=float(np.log(1e-3)), maxval=float(np.log(1e-1))))
    gdn_dt_bias = dt + jnp.log(-jnp.expm1(-dt))
    return {
        "x": x,
        "mem": mem,
        "mix_pre_g": gain((DEPTH, D_MODEL)),
        "mix_post_g": gain((DEPTH, D_MODEL)),
        "ab_w_in": nrm((N_EVEN, D_MODEL, AB_IN), D_MODEL),
        "gla_gk_w2": nrm((N_EVEN, GLA_GATE_RANK, GLA_KEY), GLA_GATE_RANK),
        "gla_gk_b": small((N_EVEN, GLA_KEY)),
        "gla_norm_g": gain((N_EVEN, GLA_DV)),
        "lru_conv_w": nrm((N_EVEN, CONV_W, LRU_WIDTH), CONV_W),
        "lru_conv_b": small((N_EVEN, LRU_WIDTH)),
        "lru_w_a": nrm((N_EVEN, LRU_BLOCKS, LRU_BLOCK, LRU_BLOCK), LRU_BLOCK),
        "lru_b_a": small((N_EVEN, LRU_WIDTH)),
        "lru_w_x": nrm((N_EVEN, LRU_BLOCKS, LRU_BLOCK, LRU_BLOCK), LRU_BLOCK),
        "lru_b_x": small((N_EVEN, LRU_WIDTH)),
        "lru_lambda": lru_lambda,
        "ab_w_out": nrm((N_EVEN, AB_MIX, D_MODEL), AB_MIX),
        "gdn_w_in": nrm((N_ODD, D_MODEL, GDN_IN), D_MODEL),
        "gdn_conv_w": nrm((N_ODD, CONV_W, GDN_CONV_CH), CONV_W),
        "gdn_a_log": gdn_a_log,
        "gdn_dt_bias": gdn_dt_bias,
        "gdn_norm_g": gain((N_ODD, GDN_DV)),
        "gdn_w_out": nrm((N_ODD, GDN_VAL, D_MODEL), GDN_VAL),
        "xa_pre_g": gain((DEPTH, D_MODEL)),
        "xa_mem_g": gain((DEPTH, D_MODEL)),
        "xa_post_g": gain((DEPTH, D_MODEL)),
        "xa_w_q": nrm((DEPTH, D_MODEL, D_MODEL), D_MODEL),
        "xa_w_kv": nrm((DEPTH, D_MODEL, 2 * D_MODEL), D_MODEL),
        "xa_w_o": nrm((DEPTH, D_MODEL, D_MODEL), D_MODEL),
        "mlp_pre_g": gain((DEPTH, D_MODEL)),
        "mlp_post_g": gain((DEPTH, D_MODEL)),
        "mlp_w1": nrm((DEPTH, D_MODEL, D_FF), D_MODEL),
        "mlp_w2": nrm((DEPTH, D_FF, D_MODEL), D_FF),
    }

def reference(x, mem, mix_pre_g, mix_post_g, ab_w_in, gla_gk_w2, gla_gk_b, gla_norm_g, lru_conv_w, lru_conv_b,
              lru_w_a, lru_b_a, lru_w_x, lru_b_x, lru_lambda, ab_w_out, gdn_w_in, gdn_conv_w, gdn_a_log, gdn_dt_bias,
              gdn_norm_g, gdn_w_out, xa_pre_g, xa_mem_g, xa_post_g, xa_w_q, xa_w_kv, xa_w_o, mlp_pre_g, mlp_post_g,
              mlp_w1, mlp_w2):
    h = x
    for i in range(DEPTH):
        j = i // 2
        hn = rms_norm(h, mix_pre_g[i])
        if i % 2 == 0:
            m = gla_lru_mixer(hn, ab_w_in[j], gla_gk_w2[j], gla_gk_b[j], gla_norm_g[j], lru_conv_w[j], lru_conv_b[j],
                              lru_w_a[j], lru_b_a[j], lru_w_x[j], lru_b_x[j], lru_lambda[j], ab_w_out[j])
        else:
            m = gdn_mixer(hn, gdn_w_in[j], gdn_conv_w[j], gdn_a_log[j], gdn_dt_bias[j], gdn_norm_g[j], gdn_w_out[j])
        h = h + rms_norm(m, mix_post_g[i])
        c = mem_cross_attn(rms_norm(h, xa_pre_g[i]), rms_norm(mem, xa_mem_g[i]), xa_w_q[i], xa_w_kv[i], xa_w_o[i])
        h = h + rms_norm(c, xa_post_g[i])
        f = sq_relu_mlp(rms_norm(h, mlp_pre_g[i]), mlp_w1[i], mlp_w2[i])
        h = h + rms_norm(f, mlp_post_g[i])
    return h


_drawn_inputs = setup_inputs


def setup_inputs(seed=0):
    import zlib

    import numpy as np

    out = dict(_drawn_inputs(seed))
    spreads = {}
    factors = {'mix_post_g': 2.738,
     'gla_gk_b': 8.0,
     'gla_norm_g': 3.265,
     'lru_b_a': 57.791,
     'lru_b_x': 28.605,
     'gdn_norm_g': 36.046,
     'xa_pre_g': 3.311,
     'xa_post_g': 3.354,
     'mlp_pre_g': 3.314,
     'mlp_post_g': 3.964}
    for name, (base, spread) in spreads.items():
        noise = np.random.default_rng([zlib.crc32(name.encode()), seed]).standard_normal(out[name].shape)
        drawn = base * np.exp(spread * noise) if base else spread * noise
        out[name] = jnp.asarray(drawn.astype(out[name].dtype))
    for name, factor in factors.items():
        out[name] = (out[name] * factor).astype(out[name].dtype)
    return out
```

```python
from contextlib import ExitStack

import concourse.bass as bass
from concourse import mybir

F32 = mybir.dt.float32
F32R = mybir.dt.float32r
U8 = mybir.dt.uint8
ALU = mybir.AluOpType
ACT = mybir.ActivationFunctionType
AX_X = mybir.AxisListType.X
ds = bass.ds

P = 128
D = 1024
SEQ = 1024
KT = D // P
HALF = 512
N_MEM = 256
CH = 128
NCH = SEQ // CH
LEVELS = 7
EPS = 1e-6
GLA_H, GLA_DK = 4, 64
LRU_T = 4
LRU_C = 8.0
GLA_GATE_NORM = 16.0
GDN_H = 8
XA_H = 4
XA_T = 2
MLP_G, MLP_T = 8, 4
CREDIT = 2

VECTORS = (("mix_pre_g", 16), ("mix_post_g", 16), ("xa_pre_g", 16), ("xa_mem_g", 16), ("xa_post_g", 16),
           ("mlp_pre_g", 16), ("mlp_post_g", 16), ("lru_conv_w", 16), ("lru_conv_b", 4), ("lru_b_a", 4),
           ("lru_b_x", 4), ("lru_lambda", 4), ("gla_gk_b", 2), ("gla_norm_g", 1), ("gdn_conv_w", 96),
           ("gdn_norm_g", 1), ("gdn_dt_bias", 8), ("gdn_a_log", 8))
COL = {name: sum(k for _, k in VECTORS[:n]) for n, (name, _) in enumerate(VECTORS)}
N_COL = sum(k for _, k in VECTORS)


class Steps:
    AHEAD = 2

    def __init__(self, sem, names):
        self.sem, self.names, self.next = sem, names.split(), 0

    def credit(self, eng):
        self.eng = eng
        eng.sem_inc(self.sem, self.AHEAD * len(self.names))

    def at(self, name, i=0):
        return (i + self.AHEAD) * len(self.names) + (self.names.index(name) + 1)

    def done(self, ins, name, i=None):
        assert self.names[self.next] == name, (self.names[self.next], name)
        self.next = (self.next + 1) % len(self.names)
        ins.then_inc(self.sem, 1)
        if i is not None:
            self.eng.wait_ge(self.sem, self.at(name, i))


class Chain:

    def __init__(self, eng, sem):
        self.eng, self.sem, self.base, self.k = eng, sem, 0, 0

    def __call__(self, ins):
        ins.then_inc(self.sem, 1)
        self.k += 1
        self.eng.wait_ge(self.sem, self.base + self.k)

    def loop(self, n, per, body):
        base, self.k = self.base + self.k, 0
        with self.eng.Fori(0, n) as i:
            self.base = i * per + base if per else base
            body(i)
            assert self.k == per, (self.k, per)
        self.base, self.k = base + n * per, 0


def schedule():
    plan, after = {}, []
    unit = 0

    def stage(name, blocks, extra=0):
        nonlocal unit
        plan[name] = (len(after), unit)
        for _ in range(blocks):
            unit += 1
            after.append(unit)
        unit += extra

    stage("mix0a", 9, extra=2 * LRU_T + 2)
    stage("mix0b", 12)
    for layer in range(2):
        if layer:
            stage("mix1", 4 * GDN_H + 1)
        stage(f"out{layer}", KT)
        stage(f"kv{layer}", 2 * KT)
        stage(f"xq{layer}", KT)
        stage(f"xo{layer}", KT)
        plan[f"mlp{layer}"] = (len(after), unit)
        for _ in range(MLP_G):
            for b in range(2 * MLP_T):
                unit += 1 + b // MLP_T
                after.append(unit)
    return plan, after


def build(nc, xT, memT, wstream, lru_w, gk_w2, pvec_in, consts_in, masks_in, outT):
    plan, after = schedule()
    NB = len(after)
    U_MLP = 3 * MLP_T
    base = (nc.sbuf_base + 63) // 64 * 64

    with ExitStack() as ctx:
        def place(name, kib, shape, dt):
            return nc.alloc_sbuf_tensor_at(name, shape, dt, offset=base + int(kib * 1024))

        def sem(name):
            return ctx.enter_context(nc.semaphore(name))

        hres = place("hres", 0, [P, KT, SEQ], F32)
        lin = place("lin", 0, [P, KT * SEQ], F32)
        act = place("act", 32, [P, KT, 2, SEQ], F32R)
        wraw = place("wraw", 96, [P, 2, D], F32)
        whl = place("whl", 104, [P, 2, 2, D], F32R)
        consts = place("consts", 120, [P, 3 * P], F32)
        masks = place("masks", 121.5, [P, 2 * LEVELS + 2, P], U8)
        pvec = place("pvec", 123.5, [P, N_COL + 2], F32)
        small = place("small", 124.75, [P, 320], F32)
        work = place("work", 126, [P, 20, SEQ], F32)
        hid = place("hid", 126 + 8 * 4, [P, MLP_T, 2, SEQ], F32R)
        memhl = place("memhl", 126 + 12 * 4, [P, 2, KT * N_MEM], F32R)
        ps = ctx.enter_context(nc.psum_tensor("ps", [P, 8, HALF], F32))
        qkvz = nc.dram_tensor("qkvz", [4, GDN_H, P, SEQ], F32, kind="Internal").ap()

        ident, ones, tri = consts[:, 0:P], consts[:, P:2 * P], consts[:, 2 * P:3 * P]
        one_col, eps_col = pvec[:, N_COL:N_COL + 1], pvec[:, N_COL + 1:N_COL + 2]
        DIAG, TRANSPOSED, CAUSAL = LEVELS, LEVELS + 1, 2 * LEVELS + 1

        def flat(ap):
            return ap.rearrange("p a n -> p (a n)")

        def unit(t, n=1):
            return flat(work[:, t:t + n, :])

        def heads(t, n=GDN_H):
            return unit(t)[:, 0:n * P].rearrange("p (h n) -> p h n", h=n)

        def heads_of(ap):
            return ap.rearrange("p (h n) -> p h n", n=P)

        def tile(buf, t):
            return flat(buf[:, ds(t, 1), :])

        def part(t, hl):
            return act[:, ds(t, 1), hl, :].rearrange("p a n -> p (a n)")

        def bank(b, n=1):
            return flat(ps[:, b:b + n, :])

        def slot(u):
            return bank(2 * (u % 2), 2)

        def col(name, k=0):
            return pvec[:, ds(k + COL[name], 1)]

        def over(ap, n):
            return ap.unsqueeze(2).to_broadcast([P, ap.shape[1], n])

        def every(ap, n):
            return ap.unsqueeze(1).to_broadcast([P, n, ap.shape[1]])

        SQ, SSQ, RSTD = 16, 18, 19

        w_in = [sem("w_in0"), sem("w_in1")]
        w_hi = sem("w_hi")
        w_split = sem("w_split")
        unit_done = sem("unit_done")
        evac = sem("evac")
        const_in, x_in, m_in, lruw_in = sem("const_in"), sem("x_in"), sem("m_in"), sem("lruw_in")
        cols_set = sem("cols_set")
        act_chain, dve_chain = sem("act_chain"), sem("dve_chain")
        act_waits, dve_waits = sem("act_waits"), sem("dve_waits")
        sq_done, sq_used = sem("sq_done"), sem("sq_used")
        stat_done, rstd_ready = sem("stat_done"), sem("rstd_ready")
        xn_ready = sem("xn_ready")
        hi_ready, act_ready = sem("hi_ready"), sem("act_ready")
        h_new = sem("h_new")
        mem_sq, mem_ssq, mem_stat, mem_rstd = sem("mem_sq"), sem("mem_ssq"), sem("mem_stat"), sem("mem_rstd")
        mem_n, mem_hi, mem_ready = sem("mem_n"), sem("mem_hi"), sem("mem_ready")
        vt_done, v_ready = sem("vt_done"), sem("v_ready")
        head_ready = sem("head_ready")
        xpe = Steps(sem("xa_pe"), "S0 T0 S1 V0 T1 V1")
        xact = Steps(sem("xa_act"), "E0 P0 E1 P1")
        xdve = Steps(sem("xa_dve"), "M0 N0 M1 O0 N1 O1")
        mlp_sq, hid_hi, hid_ready = sem("mlp_sq"), sem("hid_hi"), sem("hid_ready")
        mlp_acc = sem("mlp_acc")
        lru_conv, lru_lam, lru_in = sem("lru_conv"), sem("lru_lam"), sem("lru_in")
        lam_exp, lru_decay, lru_gain, lru_root, lru_y = (sem("lam_exp"), sem("lru_decay"), sem("lru_gain"),
                                                         sem("lru_root"), sem("lru_y"))
        gk_log, gk_part, gk_cum = sem("gk_log"), sem("gk_part"), sem("gk_cum")
        gprep = Steps(sem("gla_prep"), "sub E")
        gsel = Steps(sem("gla_select"), "m0 L0 m1 L1 m2 L2 m3 L3 S")
        gexp = Steps(sem("gla_exp"), "stage exp")
        gev = Steps(sem("gla_evac"), "tr o")
        gpe = Steps(sem("gla_pe"), "tr L0 L1 L2 L3 o s")
        o_sq, o_stat, o_rstd, o_n = sem("o_sq"), sem("o_stat"), sem("o_rstd"), sem("o_n")
        conv_done, silu_done = sem("conv_done"), sem("silu_done")
        stored = [sem("stored0"), sem("stored1")]
        loaded = [sem(f"loaded_{k}") for k in "qkvz"]
        ba_t, ba_copy, ba_sig, ba_x, ba_exp, ba_g, ba_cum, ba_done = (
            sem("ba_t"), sem("ba_copy"), sem("ba_sig"), sem("ba_x"), sem("ba_exp"), sem("ba_g"), sem("ba_cum"),
            sem("ba_done"))
        inv = range(LEVELS - 1)
        dpe = Steps(sem("gdn_pe"), "grow kt vt nrm knt ks g qk z " +
                    " ".join(f"q{n}0 q{n}1 x{n}0 x{n}1" for n in inv) + " vn o su ot")
        dact = Steps(sem("gdn_act"), "sqk sqq rk eg L LT sc knt z " + " ".join(f"q{n}0 q{n}1" for n in inv) +
                     " vn osq ro hi")
        ddve = Steps(sem("gdn_dve"), "dg m kn vb qg kd mn at x0 r " + " ".join(f"x{n}0 x{n}1" for n in inv) +
                     " o1 ss s o2 res lo")
        out_done = sem("out_done")

        def in_lin(first, *shape):
            n = 1
            for k in shape:
                n *= k
            names = "abc"[:len(shape)]
            return lin[:, first:first + n].rearrange(f"p ({' '.join(names)}) -> p {' '.join(names)}",
                                                     **dict(zip(names, shape)))

        W2, W4 = 2 * CH, 4 * CH
        gla = {
            "E": [in_lin(j * 9 * W2, 9, 2, CH) for j in range(2)],
            "QZ": [in_lin(18 * W2 + j * W4, 4, CH) for j in range(2)],
            "AT": in_lin(18 * W2 + 2 * W4, 4, CH),
            "ktok": in_lin(18 * W2 + 3 * W4, 2, CH),
            "vtok": in_lin(19 * W2 + 3 * W4, 4, CH),
            "S": in_lin(19 * W2 + 4 * W4, 2, P),
            "VS": [in_lin(20 * W2 + (4 + j) * W4, 4, CH) for j in range(2)],
            "KS": [unit(18)[:, j * W2:(j + 1) * W2].rearrange("p (h n) -> p h n", h=2) for j in range(2)],
            "QS": [unit(18)[:, (2 + j) * W2:(3 + j) * W2].rearrange("p (h n) -> p h n", h=2) for j in range(2)],
            "decay": [small[:, 308 + 2 * j:310 + 2 * j].unsqueeze(2) for j in range(2)],
        }
        gs = {name: small[:, 128 + 8 * k:128 + 8 * k + n] for name, k, n in
              (("rkq", 0, 16), ("dec", 2, 8), ("gd", 3, 8), ("egl", 4, 8), ("gl", 5, 8), ("egt", 6, 8), ("g", 7, 8),
               ("ro", 8, 8), ("oss", 9, 8), ("nb", 10, 8), ("bt", 11, 8), ("beg", 12, 8), ("rqs", 13, 8))}

        def chunks(link, prepare, finish, per):
            prepare(0, 0)

            def body(i):
                for j in range(2):
                    prepare(2 * i + (j + 1), 1 - j)
                    finish(2 * i + j, j)
            link.loop(NCH // 2 - 1, per, body)
            prepare(NCH - 1, 1)
            finish(NCH - 2, 0)
            finish(NCH - 1, 1)

        block = ctx.enter_context(nc.Block())

        @block.sync
        def _(sp):
            sp.dma_start(hres[:], xT).then_inc(x_in, 16)
            sp.dma_start(consts[:], consts_in).then_inc(const_in, 16)
            sp.dma_start(unit(14, 2), masks_in.rearrange("p m n -> p (m n)")).then_inc(const_in, 16)
            sp.dma_start(pvec[:, 0:N_COL], pvec_in).then_inc(const_in, 16)
            sp.dma_start(unit(10), lru_w).then_inc(lruw_in, 16)
            sp.dma_start(small[0:16, 0:256], gk_w2).then_inc(lruw_in, 16)
            with sp.Fori(0, NB // 2) as i:
                for j in range(2):
                    sp.wait_ge(w_split, 2 * i + (j + 1))
                    sp.dma_start(wraw[:, j, :], wstream[ds(2 * i + j, 1), :, :].rearrange("b p n -> (b p) n")) \
                        .then_inc(w_in[j], 16)
            for n in range(NB // 2 * 2, NB):
                sp.wait_ge(w_split, n + 1)
                sp.dma_start(wraw[:, n % 2, :], wstream[n]).then_inc(w_in[n % 2], 16)
            sp.wait_ge(out_done, 16 * KT)

        @block.gpsimd
        def _(pool):
            def split(n, arrived, hi_n, used):
                j = n % 2
                pool.wait_ge(unit_done, used)
                pool.wait_ge(w_in[j], arrived)
                nc.gpsimd.tensor_tensor(whl[:, j, 0, :], wraw[:, j, :], one_col.to_broadcast([P, D]),
                                        ALU.mult).then_inc(w_hi, 1)
                pool.wait_ge(w_hi, hi_n)
                nc.gpsimd.tensor_tensor(whl[:, j, 1, :], wraw[:, j, :], whl[:, j, 0, :].bitcast(F32),
                                        ALU.subtract).then_inc(w_split, 1)

            def one(n):
                split(n, 16 * (n // 2 + 1), n + 1, (after[n - 2] if n >= 2 else n - 1) + CREDIT)

            def run(n0, cnt):
                one(n0)
                one(n0 + 1)
                with pool.Fori(0, (cnt - 2) // 2) as i:
                    for n in (n0 + 2, n0 + 3):
                        split(n, 16 * i + 16 * (n // 2 + 1), 2 * i + (n + 1), 2 * i + (after[n - 2] + CREDIT))
                for n in range(n0 + cnt // 2 * 2, n0 + cnt):
                    one(n)

            def mlp(n0):
                per = 2 * MLP_T
                for n in range(n0, n0 + per):
                    one(n)
                with pool.Fori(0, MLP_G - 1) as g:
                    for n in range(n0 + per, n0 + 2 * per):
                        split(n, 8 * per * g + 16 * (n // 2 + 1), per * g + (n + 1),
                              U_MLP * g + (after[n - 2] + CREDIT))

            pool.sem_inc(w_split, CREDIT)
            nc.gpsimd.memset(one_col, 1.0).then_inc(cols_set, 1)
            nc.gpsimd.memset(eps_col, EPS).then_inc(cols_set, 1)
            pool.wait_ge(cols_set, 2)
            run(plan["mix0a"][0], 9)
            run(plan["mix0b"][0], 12)
            for layer in range(2):
                if layer:
                    run(plan["mix1"][0], 4 * GDN_H + 1)
                run(plan[f"out{layer}"][0], KT)
                run(plan[f"kv{layer}"][0], 2 * KT)
                run(plan[f"xq{layer}"][0], 2 * KT)
                mlp(plan[f"mlp{layer}"][0])

        @block.scalar
        def _(eng):
            A = nc.scalar.activation
            link = Chain(eng, act_chain)
            count = {"square": 0, "hi": 0, "norm": 0}

            def met():
                eng.sem_inc(act_waits, 1)

            def square(src, n0, i, j):
                eng.wait_ge(sq_used, 2 * i + (n0 + j + 1))
                met()
                A(unit(SQ + j), src, ACT.Square).then_inc(sq_done, 1)

            def squares_from(src, ready=None):
                n0 = KT * count["square"]
                count["square"] += 1

                def body(i):
                    for j in range(2):
                        if ready:
                            eng.wait_ge(ready[0], 2 * i + (ready[1] + j + 1))
                        square(src(2 * i + j), n0, i, j)
                link.loop(KT // 2, 0, body)

            def rstd():
                count["norm"] += 1
                eng.wait_ge(stat_done, count["norm"])
                link(A(unit(RSTD), bank(4, 2), ACT.Ln, scale=1.0 / D, bias=eps_col))
                A(unit(RSTD), unit(RSTD), ACT.Exp, scale=-0.5).then_inc(rstd_ready, 1)

            def hi_normed():
                n0 = KT * (count["norm_tiles"] if "norm_tiles" in count else 0)
                count["norm_tiles"] = n0 // KT + 1
                count["hi"] += 1

                def body(i):
                    for j in range(2):
                        eng.wait_ge(xn_ready, 2 * i + (n0 + j + 1))
                        met()
                        A(part(2 * i + j, 0), unit(SQ + j), ACT.Copy).then_inc(hi_ready, 1)
                link.loop(KT // 2, 0, body)

            def evacuate(u, u_static, out, func=ACT.Copy, **kw):
                eng.wait_ge(unit_done, u + (1 + CREDIT))
                return A(out, slot(u_static), func, **kw).then_inc(evac, 1)

            def out_epilogue(u0):
                n0 = KT * count["square"]
                count["square"] += 1

                def body(i):
                    for j in range(2):
                        eng.wait_ge(unit_done, 2 * i + (u0 + j + 1 + CREDIT))
                        square(slot(u0 + j), n0, i, j)
                        A(tile(work, 2 * i + j), slot(u0 + j), ACT.Copy).then_inc(evac, 1)
                link.loop(KT // 2, 0, body)

            def mem_norm(layer):
                eng.dma_start(unit(8, 2), memT).then_inc(m_in, 16)
                eng.wait_ge(m_in, 16 * (layer + 1))
                A(unit(10, 2), unit(8, 2), ACT.Square).then_inc(mem_sq, 1)
                eng.wait_ge(mem_stat, layer + 1)
                link(A(small[:, 0:N_MEM], bank(7)[:, 0:N_MEM], ACT.Ln, scale=1.0 / D, bias=eps_col))
                A(small[:, 0:N_MEM], small[:, 0:N_MEM], ACT.Exp, scale=-0.5).then_inc(mem_rstd, 1)
                eng.wait_ge(mem_n, layer + 1)
                A(memhl[:, 0, :], unit(8, 2), ACT.Copy).then_inc(mem_hi, 1)

            def residual_squares_and_kv(layer, h0):
                u0 = plan[f"kv{layer}"][1]
                n0 = KT * count["square"]
                count["square"] += 1
                kv = unit(8, 4).rearrange("p (t m) -> p t m", m=N_MEM)
                eng.wait_ge(mem_ready, layer + 1)

                def body(i):
                    for j in range(2):
                        for k in (2 * j, 2 * j + 1):
                            eng.wait_ge(unit_done, 4 * i + (u0 + k + 1 + CREDIT))
                            met()
                            A(flat(kv[:, ds(4 * i + k, 1), :]), slot(u0 + k)[:, 0:N_MEM], ACT.Copy) \
                                .then_inc(evac, 1)
                        eng.wait_ge(h_new, 2 * i + (h0 + j + 1))
                        square(tile(hres, 2 * i + j), n0, i, j)
                link.loop(KT // 2, 0, body)

            def attention(layer):
                u0 = plan[f"xq{layer}"][1]
                qh = work[:, 10:12, :]
                vh = unit(SSQ)[:, 0:2 * N_MEM].rearrange("p (m d) -> p m d", m=2)
                v = work[:, 12:14, :]
                p, pt = unit(14), unit(15)
                mx, den = small[:, 256:264], small[:, 264:272]
                eng.wait_ge(v_ready, 4 * (layer + 1))

                def body(h):
                    k = h + XA_H * layer
                    eng.wait_ge(xpe.sem, xpe.at("V1", k - 1))
                    for d in range(XA_T):
                        evacuate(XA_T * h + (u0 + d), u0 + d, qh[:, d, :], scale=float(XA_T * P) ** -0.5)
                    A(vh, v[:, :, ds(h * N_MEM, N_MEM)], ACT.Copy).then_inc(head_ready, 1)
                    for e in range(2):
                        eng.wait_ge(xdve.sem, xdve.at(f"M{e}", k))
                        eng.wait_ge(xpe.sem, xpe.at("T0", k) if e else xpe.at("T1", k - 1))
                        for j in range(4):
                            at = slice(j * N_MEM, (j + 1) * N_MEM)
                            last = A(p[:, at], bank(4, 2)[:, at], ACT.Exp, bias=mx[:, 4 * e + j:4 * e + j + 1],
                                     accum_out=den[:, 4 * e + j:4 * e + j + 1])
                        xact.done(last, f"E{e}", k)
                        eng.wait_ge(xpe.sem, xpe.at(f"T{e}", k))
                        xact.done(A(pt, bank(6, 2), ACT.Copy), f"P{e}", k)
                link.loop(XA_H, 0, body)

            def split_hi(layer):
                count["hi"] += 1
                eng.wait_ge(xdve.sem, xdve.at("O1", XA_H * (layer + 1) - 1))

                def body(i):
                    for j in range(2):
                        A(part(2 * i + j, 0), tile(work, 2 * i + j), ACT.Copy).then_inc(hi_ready, 1)
                link.loop(KT // 2, 0, body)

            def mlp(layer):
                u0 = plan[f"mlp{layer}"][1]

                def body(g):
                    h0 = MLP_T * MLP_G * layer
                    for t in range(MLP_T):
                        eng.wait_ge(mlp_acc, 2 * MLP_T * g + (2 * h0 + t + 1))
                        evacuate(U_MLP * g + (u0 + t), u0 + t, unit(SQ + t), ACT.Relu)
                    for t in range(MLP_T):
                        eng.wait_ge(mlp_sq, MLP_T * g + (h0 + t + 1))
                        A(hid[:, t, 0, :], unit(SQ + t), ACT.Copy).then_inc(hid_hi, 1)
                    for t in range(2 * MLP_T):
                        if t < MLP_T:
                            eng.wait_ge(hid_ready, MLP_T * g + (h0 + t + 1))
                        else:
                            eng.wait_ge(mlp_acc, 2 * MLP_T * g + (2 * h0 + t + 1))
                        evacuate(U_MLP * g + (u0 + MLP_T + t), u0 + MLP_T + t, unit(SQ + t % MLP_T))
                link.loop(MLP_G, 0, body)

            def store_tile(i, j, h0):
                eng.wait_ge(h_new, 2 * i + (h0 + j + 1))
                eng.dma_start(outT[:, ds(2 * i + j, 1), :].rearrange("p a n -> p (a n)"),
                              tile(hres, 2 * i + j)).then_inc(out_done, 16)

            def mixer0():
                ua, ub = plan["mix0a"][1], plan["mix0b"][1]
                R, I = (lambda t: lin[:, t * SEQ:(t + 1) * SEQ]), (lambda t: lin[:, (4 + t) * SEQ:(5 + t) * SEQ])
                link(A(small[:, 284:288], pvec[:, COL["lru_lambda"]:COL["lru_lambda"] + 4], ACT.Abs))
                A(small[:, 284:288], small[:, 284:288], ACT.Exp, scale=-1.0).then_inc(lam_exp, 1)
                for t in range(LRU_T):
                    if t >= 2:
                        eng.wait_ge(lru_conv, t - 1)
                    evacuate(ua + t, ua + t, unit(8 + t % 2))
                for t in range(LRU_T):
                    evacuate(ua + 4 + t, ua + 4 + t, unit(4 + t), ACT.Gelu_apprx_tanh)
                evacuate(ua + 8, ua + 8, unit(11))
                for t in range(LRU_T):
                    u = ua + 9 + 2 * t
                    evacuate(u, u, R(t), ACT.Sigmoid, bias=col("lru_b_a", t))
                    evacuate(u + 1, u + 1, I(t), ACT.Sigmoid, bias=col("lru_b_x", t))
                for hp in range(2):
                    u, gk = ua + 9 + 2 * LRU_T + hp, unit(16 + hp)
                    evacuate(u, u, gk, ACT.Identity, bias=col("gla_gk_b", hp))
                    eng.wait_ge(evac, u + 1 + CREDIT)
                    if hp:
                        eng.wait_ge(gk_part, 1)
                    link(A(unit(18), gk, ACT.Abs))
                    link(A(unit(18), unit(18), ACT.Exp, scale=-1.0))
                    A(unit(18), unit(18), ACT.Ln, bias=one_col).then_inc(gk_log, 1)
                eng.wait_ge(lru_conv, LRU_T)
                for t in range(GLA_H):
                    evacuate(ub + t, ub + t, unit(8 + t))
                eng.wait_ge(lru_lam, 1)
                for t in range(LRU_T):
                    eng.wait_ge(lru_in, t + 1)
                    A(unit(t), R(t), ACT.Exp, scale=small[:, 300 + t:301 + t])
                    A(R(t), R(t), ACT.Tanh, scale=small[:, 304 + t:305 + t]).then_inc(lru_decay, 1)
                for t in range(GLA_H):
                    evacuate(ub + 4 + t, ub + 4 + t, unit(12 + t), ACT.Silu)
                for t in range(LRU_T):
                    eng.wait_ge(lru_gain, t + 1)
                    A(R(t), R(t), ACT.Sqrt).then_inc(lru_root, 1)
                eng.wait_ge(lru_y, LRU_T)
                for t in range(2):
                    evacuate(ub + 8 + t, ub + 8 + t, unit(4 + t), scale=float(GLA_DK) ** -0.5)
                for t in range(2):
                    evacuate(ub + 10 + t, ub + 10 + t, unit(6 + t))
                eng.wait_ge(evac, ub + 12 + CREDIT)

                def prepare(c, j):
                    e, vs, ks = gla["E"][j], gla["VS"][j], gla["KS"][j]
                    eng.wait_ge(gpe.sem, gpe.at("L3", c - 2))
                    met()
                    A(vs, work[:, 8:12, ds(c * CH, CH)], ACT.Copy)
                    A(gla["QS"][j], work[:, 4:6, ds(c * CH, CH)], ACT.Copy)
                    gexp.done(A(ks, work[:, 6:8, ds(c * CH, CH)], ACT.Copy), "stage", c)
                    eng.wait_ge(gprep.sem, gprep.at("sub", c))
                    eng.wait_ge(gsel.sem, gsel.at("S", c - 2))
                    A(e[:, 0:8], e[:, 0:8], ACT.Exp)
                    A(e[:, 8], work[:, 16:18, ds(c * CH, CH)], ACT.Exp)
                    gexp.done(A(gla["decay"][j], work[:, 16:18, ds(c * CH + (CH - 1), 1)], ACT.Exp), "exp", c)

                def finish(c, j):
                    eng.wait_ge(gpe.sem, gpe.at("tr", c))
                    A(gla["ktok"], bank(5)[:, 0:2 * P].rearrange("p (h n) -> p h n", h=2), ACT.Copy)
                    gev.done(A(gla["vtok"], bank(4).rearrange("p (h n) -> p h n", h=4), ACT.Copy), "tr", c)
                    eng.wait_ge(gpe.sem, gpe.at("o", c))
                    met()
                    gev.done(A(work[:, 8:12, ds(c * CH, CH)], bank(6).rearrange("p (h n) -> p h n", h=4), ACT.Copy),
                             "o", c)

                chunks(link, prepare, finish, 0)
                count["hi"] += 1
                for t in range(LRU_T):
                    A(part(t, 0), unit(t), ACT.Copy).then_inc(hi_ready, 1)
                eng.wait_ge(gsel.sem, gsel.at("S", NCH - 1))
                eng.dma_start(hres[:], xT).then_inc(x_in, 16)
                eng.wait_ge(gev.sem, gev.at("o", NCH - 1))
                for h in range(GLA_H):
                    A(unit(4 + h), unit(8 + h), ACT.Square).then_inc(o_sq, 1)
                for h in range(GLA_H):
                    eng.wait_ge(o_stat, h + 1)
                    link(A(unit(4 + h), slot(h), ACT.Ln, scale=1.0 / P, bias=eps_col))
                    A(unit(4 + h), unit(4 + h), ACT.Exp, scale=-0.5).then_inc(o_rstd, 1)
                for h in range(GLA_H):
                    eng.wait_ge(o_n, h + 1)
                    A(part(LRU_T + h, 0), unit(8 + h), ACT.Copy).then_inc(hi_ready, 1)
                eng.wait_ge(act_ready, 2 * KT)

            def mixer1():
                u0 = plan["mix1"][1]
                eng.sem_inc(stored[0], 16)
                eng.sem_inc(stored[1], 16)
                eng.sem_inc(silu_done, 3)

                def store(kind, h, s):
                    eng.dma_start(qkvz[kind, ds(h, 1), :, :].rearrange("h p n -> (h p) n"),
                                  unit(2 + s)).then_inc(stored[s], 16)

                def body(h):
                    def silu(k, s, nth):
                        eng.wait_ge(conv_done, 3 * h + (k + 1))
                        eng.wait_ge(stored[s], 32 * h + (16 * nth + 16))
                        A(unit(2 + s), unit(4 + k), ACT.Silu).then_inc(silu_done, 1)
                        eng.wait_ge(silu_done, 3 * h + (k + 1 + 3))
                        store(k, h, s)

                    evacuate(4 * h + u0, u0, unit(0))
                    evacuate(4 * h + (u0 + 1), u0 + 1, unit(1))
                    silu(0, 0, 0)
                    evacuate(4 * h + (u0 + 2), u0 + 2, unit(0))
                    silu(1, 1, 0)
                    eng.wait_ge(stored[0], 32 * h + 32)
                    evacuate(4 * h + (u0 + 3), u0 + 3, unit(2), ACT.Silu)
                    eng.wait_ge(evac, 4 * h + (u0 + 4 + CREDIT))
                    store(3, h, 0)
                    silu(2, 1, 1)
                link.loop(GDN_H, 0, body)
                ub = u0 + 4 * GDN_H
                evacuate(ub, ub, unit(7))
                eng.wait_ge(ba_copy, 1)
                beta = small[:, 64:128].rearrange("p (c h) -> p c h", c=NCH)
                ba = unit(6)[:, 0:128].rearrange("p (c k) -> p c k", c=NCH)
                A(beta, ba[:, :, 0:GDN_H], ACT.Sigmoid).then_inc(ba_sig, 1)
                eng.wait_ge(ba_x, 1)
                A(unit(6)[:, 192:256], unit(6)[:, 128:192], ACT.Abs).then_inc(ba_sig, 1)
                eng.wait_ge(ba_sig, 2)
                A(unit(6)[:, 192:256], unit(6)[:, 192:256], ACT.Exp, scale=-1.0)
                A(unit(6)[:, 256:264], pvec[:, COL["gdn_a_log"]:COL["gdn_a_log"] + 8], ACT.Exp).then_inc(ba_exp, 1)
                for s in range(2):
                    eng.wait_ge(stored[s], 16 + 32 * GDN_H)

                def chunk(c):
                    W = (lambda name, i=c: eng.wait_ge(ddve.sem, ddve.at(name, i)))
                    Wp = (lambda name, i=c: eng.wait_ge(dpe.sem, dpe.at(name, i)))
                    W("lo", c - 1)
                    for kind in (1, 0, 2, 3):
                        eng.dma_start(heads(kind), qkvz[kind, :, :, ds(c * CH, CH)].rearrange("h p n -> p h n")) \
                            .then_inc(loaded[kind], 16)
                    eng.wait_ge(loaded[1], 16 * c + 16)
                    dact.done(A(unit(19), unit(1), ACT.Square), "sqk", c)
                    eng.wait_ge(loaded[0], 16 * c + 16)
                    dact.done(A(unit(14), unit(0), ACT.Square), "sqq", c)
                    Wp("nrm")
                    link(A(gs["rkq"], bank(6)[:, 0:16], ACT.Ln, bias=eps_col))
                    dact.done(A(gs["rkq"], gs["rkq"], ACT.Exp, scale=-0.5), "rk", c)
                    W("m")
                    dact.done(A(unit(18), bank(0, 2), ACT.Exp), "eg", c)
                    dact.done(A(unit(5), unit(5), ACT.Exp), "L", c)
                    dact.done(A(unit(6), unit(6), ACT.Exp, scale=-1.0), "LT", c)
                    A(gs["dec"], gs["gd"], ACT.Exp)
                    A(gs["egl"], gs["gl"], ACT.Exp)
                    dact.done(A(gs["egt"], gs["g"], ACT.Exp), "sc", c)
                    Wp("knt")
                    dact.done(A(unit(8), bank(2, 2), ACT.Copy), "knt", c)
                    Wp("z")
                    dact.done(A(unit(13), bank(2, 2), ACT.Copy), "z", c)
                    for n in inv:
                        for g in range(2):
                            Wp(f"q{n}{g}")
                            dact.done(A(unit(14)[:, g * HALF:(g + 1) * HALF], bank(g), ACT.Copy), f"q{n}{g}", c)
                    Wp("vn")
                    dact.done(A(unit(16), bank(0, 2), ACT.Copy), "vn", c)
                    W("o1")
                    dact.done(A(unit(14), unit(19), ACT.Square), "osq", c)
                    W("ss")
                    link(A(gs["ro"], gs["oss"], ACT.Ln, scale=1.0 / P, bias=eps_col))
                    dact.done(A(gs["ro"], gs["ro"], ACT.Exp, scale=-0.5), "ro", c)
                    W("res")
                    met()
                    dact.done(A(act[:, :, 0, ds(c * CH, CH)], heads(19), ACT.Copy), "hi", c)
                link.loop(NCH, 2, chunk)

            eng.sem_inc(evac, CREDIT)
            for s in (xact, gexp, gev, dact):
                s.credit(eng)
            eng.wait_ge(const_in, 48)
            eng.wait_ge(cols_set, 2)
            eng.wait_ge(x_in, 16)
            squares_from(lambda t: tile(hres, t))
            rstd()
            hi_normed()
            mixer0()
            for layer in range(2):
                h0 = 3 * KT * layer
                if layer:
                    rstd()
                    squares_from(lambda t: tile(hres, t), (h_new, 2 * KT))
                    rstd()
                    hi_normed()
                    mixer1()
                mem_norm(layer)
                out_epilogue(plan[f"out{layer}"][1])
                rstd()
                residual_squares_and_kv(layer, h0)
                rstd()
                hi_normed()
                attention(layer)
                split_hi(layer)
                out_epilogue(plan[f"xo{layer}"][1])
                rstd()
                squares_from(lambda t: tile(hres, t), (h_new, h0 + KT))
                rstd()
                hi_normed()
                mlp(layer)
                eng.wait_ge(mlp_acc, 2 * (layer + 1) * MLP_T * MLP_G + MLP_T)
                squares_from(lambda t: tile(work, t))
            rstd()
            link.loop(KT // 2, 0, lambda i: [store_tile(i, j, 5 * KT) for j in range(2)])

        @block.vector
        def _(eng):
            V = nc.vector
            TT, TS, STT = V.tensor_tensor, V.tensor_scalar, V.scalar_tensor_tensor
            link = Chain(eng, dve_chain)
            count = {"square": 0, "hi": 0, "norm": 0}

            def met():
                eng.sem_inc(dve_waits, 1)

            def add_square(n0, i, j):
                eng.wait_ge(sq_done, 2 * i + (n0 + j + 1))
                eng.wait_ge(sq_used, 2 * i + (n0 + j + CREDIT))
                TT(unit(SSQ), unit(SSQ), unit(SQ + j), ALU.add).then_inc(sq_used, 1)

            def sum_squares():
                n0 = KT * count["square"]
                count["square"] += 1
                link(V.memset(unit(SSQ), 0.0))

                def body(i):
                    for j in range(2):
                        add_square(n0, i, j)
                link.loop(KT // 2, 0, body)

            def wait_rstd():
                count["norm"] += 1
                eng.wait_ge(rstd_ready, count["norm"])

            def residual(gain, k0, squares=True):
                wait_rstd()
                n0 = KT * count["square"]
                if squares:
                    count["square"] += 1
                    link(V.memset(unit(SSQ), 0.0))

                def body(i):
                    for j in range(2):
                        m = tile(work, 2 * i + j)
                        link(STT(out=m, in0=m, scalar=col(gain, 2 * i + (k0 + j)), in1=unit(RSTD), op0=ALU.mult,
                                 op1=ALU.mult))
                    for j in range(2):
                        h = tile(hres, 2 * i + j)
                        TT(h, h, tile(work, 2 * i + j), ALU.add).then_inc(h_new, 1)
                    if squares:
                        for j in range(2):
                            add_square(n0, i, j)
                link.loop(KT // 2, 2, body)

            def lo_part(t, src, n0, i, j):
                eng.wait_ge(hi_ready, 2 * i + (n0 + j + 1))
                TT(part(t, 1), src, part(t, 0).bitcast(F32), ALU.subtract).then_inc(act_ready, 1)
                eng.wait_ge(act_ready, 2 * i + (n0 + j + 1))

            def normed(gain, k0):
                wait_rstd()
                n0 = KT * count["hi"]
                count["hi"] += 1

                def body(i):
                    for j in range(2):
                        STT(out=unit(SQ + j), in0=tile(hres, 2 * i + j), scalar=col(gain, 2 * i + (k0 + j)),
                            in1=unit(RSTD), op0=ALU.mult, op1=ALU.mult).then_inc(xn_ready, 1)
                    for j in range(2):
                        lo_part(2 * i + j, unit(SQ + j), n0, i, j)
                link.loop(KT // 2, 0, body)

            def convolve(x, out, w, bias, done):
                if bias is None:
                    link(TS(out, x, w(3), None, ALU.mult))
                else:
                    link(TS(out, x, w(3), bias, ALU.mult, ALU.add))
                for back in (1, 2, 3):
                    ins = STT(out=out[:, back:], in0=x[:, 0:SEQ - back], scalar=w(3 - back), in1=out[:, back:],
                              op0=ALU.mult, op1=ALU.add)
                    if back < 3:
                        link(ins)
                ins.then_inc(done, 1)

            def log1p(e, out, s, s2):
                link(TS(s, e, 2.0, None, ALU.add))
                link(V.reciprocal(s, s))
                link(TT(s, s, e, ALU.mult))
                link(TT(s2, s, s, ALU.mult))
                link(TS(out, s2, 1.0 / 17, None, ALU.mult))
                for k in range(15, 1, -2):
                    link(STT(out=out, in0=out, scalar=1.0 / k, in1=s2, op0=ALU.add, op1=ALU.mult))
                link(STT(out=out, in0=out, scalar=1.0, in1=s, op0=ALU.add, op1=ALU.mult))
                link(TS(out, out, 2.0, None, ALU.mult))

            def mem_norm(layer):
                eng.wait_ge(mem_sq, layer + 1)
                V.tensor_reduce(small[:, 0:N_MEM], unit(10, 2).rearrange("p (k m) -> p m k", k=KT), AX_X,
                                ALU.add).then_inc(mem_ssq, 1)
                eng.wait_ge(mem_rstd, layer + 1)
                for k in range(KT):
                    m = unit(8, 2)[:, k * N_MEM:(k + 1) * N_MEM]
                    last = STT(out=m, in0=m, scalar=col("xa_mem_g", KT * layer + k), in1=small[:, 0:N_MEM],
                               op0=ALU.mult, op1=ALU.mult)
                last.then_inc(mem_n, 1)
                eng.wait_ge(mem_hi, layer + 1)
                TT(memhl[:, 1, :], unit(8, 2), memhl[:, 0, :].bitcast(F32), ALU.subtract).then_inc(mem_ready, 1)

            def values(layer):
                eng.wait_ge(vt_done, layer + 1)
                for m in range(2):
                    for k in range(2):
                        V.tensor_copy(unit(12 + m)[:, k * HALF:(k + 1) * HALF], bank(4 + 2 * m + k)) \
                            .then_inc(v_ready, 1)

            def attention(layer):
                mx, den, rd = small[:, 256:264], small[:, 264:272], small[:, 272:280]
                s4 = bank(4, 2).rearrange("p (t m) -> p t m", t=4)
                p4 = unit(14).rearrange("p (t m) -> p t m", t=4)

                def body(h):
                    k = h + XA_H * layer

                    def maxima(e):
                        eng.wait_ge(xpe.sem, xpe.at(f"S{e}", k))
                        m = mx[:, 4 * e:4 * e + 4]
                        link(V.tensor_reduce(m, s4, AX_X, ALU.max))
                        xdve.done(TS(m, m, -1.0, None, ALU.mult), f"M{e}", k)

                    def normalise(e):
                        eng.wait_ge(xact.sem, xact.at(f"E{e}", k))
                        r = rd[:, 4 * e:4 * e + 4]
                        link(V.reciprocal(r, den[:, 4 * e:4 * e + 4]))
                        xdve.done(TT(p4, p4, over(r, N_MEM), ALU.mult), f"N{e}", k)

                    def output(e):
                        eng.wait_ge(xpe.sem, xpe.at(f"V{e}", k))
                        xdve.done(V.tensor_copy(work[:, ds(XA_T * h, XA_T), e * HALF:(e + 1) * HALF], ps[:, 6:8, :]),
                                  f"O{e}", k)

                    maxima(0)
                    normalise(0)
                    maxima(1)
                    output(0)
                    normalise(1)
                    output(1)
                link.loop(XA_H, 4, body)

            def split_lo():
                n0 = KT * count["hi"]
                count["hi"] += 1

                def body(i):
                    for j in range(2):
                        lo_part(2 * i + j, tile(work, 2 * i + j), n0, i, j)
                link.loop(KT // 2, 0, body)

            def mlp(layer):
                u0 = plan[f"mlp{layer}"][1]
                h0 = MLP_T * MLP_G * layer
                link(V.memset(work[:, 0:8, :], 0.0))

                def body(g):
                    for t in range(MLP_T):
                        eng.wait_ge(evac, U_MLP * g + (u0 + t + 1 + CREDIT))
                        TT(unit(SQ + t), unit(SQ + t), unit(SQ + t), ALU.mult).then_inc(mlp_sq, 1)
                    for t in range(MLP_T):
                        eng.wait_ge(hid_hi, MLP_T * g + (h0 + t + 1))
                        TT(hid[:, t, 1, :], unit(SQ + t), hid[:, t, 0, :].bitcast(F32), ALU.subtract) \
                            .then_inc(hid_ready, 1)
                    for t in range(2 * MLP_T):
                        eng.wait_ge(evac, U_MLP * g + (u0 + MLP_T + t + 1 + CREDIT))
                        eng.wait_ge(mlp_acc, 2 * MLP_T * g + (2 * h0 + t + MLP_T))
                        TT(unit(t), unit(t), unit(SQ + t % MLP_T), ALU.add).then_inc(mlp_acc, 1)
                link.loop(MLP_G, 0, body)

            def mixer0():
                ua = plan["mix0a"][1]
                R, I = (lambda t: lin[:, t * SEQ:(t + 1) * SEQ]), (lambda t: lin[:, (4 + t) * SEQ:(5 + t) * SEQ])
                lam = pvec[:, COL["lru_lambda"]:COL["lru_lambda"] + 4]
                eng.wait_ge(lam_exp, 1)
                log1p(small[:, 284:288], small[:, 288:292], small[:, 292:296], small[:, 296:300])
                link(TS(small[:, 292:296], lam, -1.0, 0.0, ALU.mult, ALU.max))
                link(TT(small[:, 288:292], small[:, 288:292], small[:, 292:296], ALU.add))
                TS(small[:, 300:304], small[:, 288:292], -LRU_C, None, ALU.mult)
                TS(small[:, 304:308], small[:, 288:292], LRU_C, None, ALU.mult).then_inc(lru_lam, 1)
                for t in range(LRU_T):
                    eng.wait_ge(evac, ua + t + 1 + CREDIT)
                    convolve(unit(8 + t % 2), unit(t), lambda k: col("lru_conv_w", 4 * t + k), col("lru_conv_b", t),
                             lru_conv)
                for t in range(LRU_T):
                    eng.wait_ge(evac, ua + 9 + 2 * t + 2 + CREDIT)
                    TT(I(t), I(t), unit(t), ALU.mult).then_inc(lru_in, 1)
                for hp in range(2):
                    gk = unit(16 + hp)
                    eng.wait_ge(gk_log, hp + 1)
                    link(TS(gk, gk, 0.0, 1.0 / GLA_GATE_NORM, ALU.min, ALU.mult))
                    STT(out=gk, in0=unit(18), scalar=-1.0 / GLA_GATE_NORM, in1=gk, op0=ALU.mult, op1=ALU.add) \
                        .then_inc(gk_part, 1)
                    eng.wait_ge(gk_part, hp + 1)

                    def scan(c):
                        b = gk[:, ds(c * CH, CH)]
                        V.tensor_tensor_scan(b, ones, b, 0.0, ALU.mult, ALU.add).then_inc(gk_cum, 1)
                    link.loop(NCH, 0, scan)
                for t in range(LRU_T):
                    eng.wait_ge(lru_decay, t + 1)
                    link(TT(unit(19), unit(t), unit(t), ALU.mult))
                    STT(out=R(t), in0=unit(19), scalar=1.0, in1=R(t), op0=ALU.add, op1=ALU.mult) \
                        .then_inc(lru_gain, 1)
                    eng.wait_ge(lru_gain, t + 1)
                for t in range(LRU_T):
                    eng.wait_ge(lru_root, t + 1)
                    link(TT(I(t), I(t), R(t), ALU.mult))
                    link(V.tensor_tensor_scan(R(t), unit(t), I(t), 0.0, ALU.mult, ALU.add))
                    TT(unit(t), R(t), unit(4 + t), ALU.mult).then_inc(lru_y, 1)
                eng.wait_ge(lru_y, LRU_T)
                for buf in (*gla["QZ"], gla["AT"], gla["S"]):
                    link(V.memset(buf, 0.0))
                eng.wait_ge(gk_cum, 2 * NCH)
                eng.wait_ge(evac, plan["mix0b"][1] + 12 + CREDIT)

                def halves(ap, level):
                    half = CH >> (level + 1)
                    v = ap.rearrange("p h (n s t) -> p h n s t", s=2, t=half)
                    return v[:, :, :, 0, :], v[:, :, :, 1, :]

                def prepare(c, j):
                    e, qz = gla["E"][j], gla["QZ"][j]
                    q, k, b = (work[:, t:t + 2, ds(c * CH, CH)] for t in (4, 6, 16))
                    eng.wait_ge(gpe.sem, gpe.at("o", c - 2))
                    for level in range(LEVELS):
                        b_lo, b_up = halves(b, level)
                        e_lo, e_up = halves(e[:, level], level)
                        ref = b_lo[:, :, :, b_lo.shape[3] - 1:b_lo.shape[3]].to_broadcast(list(b_lo.shape))
                        TT(e_lo, ref, b_lo, ALU.subtract)
                        TT(e_up, b_up, ref, ALU.subtract)
                    gprep.done(TT(e[:, 7], b[:, :, CH - 1:CH].to_broadcast([P, 2, CH]), b, ALU.subtract), "sub", c)
                    eng.wait_ge(gexp.sem, gexp.at("exp", c))
                    for level in range(LEVELS):
                        e_lo, e_up = halves(e[:, level], level)
                        TT(e_lo, e_lo, halves(k, level)[0], ALU.mult)
                        TT(e_up, e_up, halves(q, level)[1], ALU.mult)
                    TT(e[:, 7], e[:, 7], k, ALU.mult)
                    for par in range(2):
                        rows = slice(64 * par, 64 * par + 64)
                        out = qz.rearrange("p (h r) n -> p h r n", r=2)[rows, :, par, :]
                        last = TT(out, e[rows, 8], q[rows], ALU.mult)
                    gprep.done(last, "E", c)

                def finish(c, j):
                    at4 = gla["AT"].rearrange("p (a b) n -> p a b n", a=2)
                    eng.wait_ge(gpe.sem, gpe.at("o", c - 1))
                    for pair in range(4):
                        eng.wait_ge(gpe.sem, gpe.at(f"L{pair}", c))
                        met()
                        for lv in range(2):
                            mask = masks[:, 2 * pair + lv, :].unsqueeze(1).unsqueeze(1).to_broadcast([P, 2, 2, CH])
                            data = ps[:, 2 * (pair % 2):2 * (pair % 2) + 2, lv * W2:(lv + 1) * W2] \
                                .rearrange("p a (b n) -> p a b n", b=2)
                            gsel.done(V.copy_predicated(at4, mask, data), f"L{pair}" if lv else f"m{pair}", c)
                            if not lv:
                                met()
                    eng.wait_ge(gpe.sem, gpe.at("s", c))
                    eng.wait_ge(gsel.sem, gsel.at("S", c - 1))
                    for hp in range(2):
                        s = gla["S"][:, hp, :]
                        last = STT(out=s, in0=s, scalar=gla["decay"][j][:, hp, :], in1=bank(7)[:, hp * P:(hp + 1) * P],
                                   op0=ALU.mult, op1=ALU.add)
                    gsel.done(last, "S", c)

                chunks(link, prepare, finish, 0)
                n0 = KT * count["hi"]
                count["hi"] += 1
                for t in range(LRU_T):
                    eng.wait_ge(hi_ready, n0 + t + 1)
                    TT(part(t, 1), unit(t), part(t, 0).bitcast(F32), ALU.subtract).then_inc(act_ready, 1)
                for h in range(GLA_H):
                    eng.wait_ge(o_rstd, h + 1)
                    o = unit(8 + h)
                    link(STT(out=o, in0=o, scalar=col("gla_norm_g"), in1=unit(4 + h), op0=ALU.mult, op1=ALU.mult))
                    TT(o, o, unit(12 + h), ALU.mult).then_inc(o_n, 1)
                for h in range(GLA_H):
                    eng.wait_ge(hi_ready, n0 + LRU_T + h + 1)
                    TT(part(LRU_T + h, 1), unit(8 + h), part(LRU_T + h, 0).bitcast(F32), ALU.subtract) \
                        .then_inc(act_ready, 1)

            def mixer1():
                u0 = plan["mix1"][1]

                def body(h):
                    for k in range(3):
                        eng.wait_ge(evac, 4 * h + (u0 + k + 1 + CREDIT))
                        eng.wait_ge(silu_done, 3 * h + (k + 1))
                        convolve(unit(k % 2), unit(4 + k), lambda tap: col("gdn_conv_w", 4 * h + (32 * k + tap)),
                                 None, conv_done)
                link.loop(GDN_H, 9, body)
                t6 = unit(6)

                def grid(first, n=8):
                    return t6[:, first:first + NCH * n].rearrange("p (c k) -> p c k", c=NCH)

                eng.wait_ge(ba_t, 1)
                V.tensor_copy(grid(0, 16), heads_of(bank(4, 2))[:, :, 0:16]).then_inc(ba_copy, 1)
                eng.wait_ge(ba_copy, 1)
                dt = pvec[:, COL["gdn_dt_bias"]:COL["gdn_dt_bias"] + 8]
                TT(grid(128), grid(0, 16)[:, :, 8:16], every(dt, NCH), ALU.add).then_inc(ba_x, 1)
                eng.wait_ge(ba_exp, 1)
                log1p(t6[:, 192:256], t6[:, 320:384], t6[:, 384:448], t6[:, 448:512])
                link(TS(t6[:, 128:192], t6[:, 128:192], 0.0, None, ALU.max))
                link(TT(t6[:, 320:384], t6[:, 320:384], t6[:, 128:192], ALU.add))
                link(TT(grid(320), grid(320), every(t6[:, 256:264], NCH), ALU.mult))
                TS(t6[:, 512:576], t6[:, 320:384], -1.0, None, ALU.mult).then_inc(ba_g, 1)
                eng.wait_ge(ba_cum, 1)
                link(V.tensor_copy(small[:, 0:64], bank(6)[:, 0:64]))
                link(V.memset(unit(15), 0.0))
                eng.wait_ge(ba_sig, 2)

                def chunk(c):
                    Wa = (lambda name: eng.wait_ge(dact.sem, dact.at(name, c)))
                    Wp = (lambda name: eng.wait_ge(dpe.sem, dpe.at(name, c)))
                    g, L, LT, S = heads(4), heads(5), heads(6), heads(15)
                    X, Z = heads(12), heads(13)
                    V.tensor_copy(gs["g"], small[:, ds(c * GDN_H, GDN_H)])
                    link(V.tensor_copy(gs["bt"], small[:, ds(c * GDN_H + 64, GDN_H)]))
                    TS(gs["nb"], gs["bt"], -1.0, None, ALU.mult)
                    ddve.done(TT(g, every(ident, GDN_H), over(gs["g"], CH), ALU.mult), "dg", c)
                    Wp("grow")
                    grow = heads_of(bank(0, 2))
                    V.tensor_copy(gs["gl"], grow[:, :, CH - 1:CH].rearrange("p h o -> p (h o)"))
                    link(TT(g, over(gs["g"], CH), grow, ALU.subtract))
                    TT(gs["gd"], gs["gl"], gs["g"], ALU.subtract)
                    TS(unit(5), unit(4), 0.0, None, ALU.min)
                    ddve.done(TS(unit(6), unit(4), 0.0, None, ALU.max), "m", c)
                    Wp("kt")
                    Wa("rk")
                    TS(gs["rqs"], gs["rkq"][:, 8:16], float(P) ** -0.5, None, ALU.mult)
                    ddve.done(TT(heads(7), heads_of(bank(2, 2)), over(gs["rkq"][:, 0:8], P), ALU.mult), "kn", c)
                    Wp("vt")
                    ddve.done(TT(heads(9), heads_of(bank(4, 2)), over(gs["bt"], P), ALU.mult), "vb", c)
                    Wa("eg")
                    ddve.done(TT(unit(18), unit(18), unit(0), ALU.mult), "qg", c)
                    Wa("sc")
                    TT(gs["beg"], gs["bt"], gs["egt"], ALU.mult)
                    ddve.done(TT(heads(17), heads(7), over(gs["dec"], P), ALU.mult), "kd", c)
                    TT(L, L, over(gs["nb"], CH), ALU.mult)
                    link(TT(LT, LT, every(masks[:, CAUSAL, :], GDN_H), ALU.mult))
                    Wp("g")
                    ddve.done(TT(unit(10), bank(0, 2), unit(5), ALU.mult), "mn", c)
                    Wp("qk")
                    ddve.done(TT(unit(11), bank(4, 2), unit(6), ALU.mult), "at", c)
                    link(V.tensor_copy(X, every(ident, GDN_H)))
                    met()
                    ddve.done(V.copy_predicated(X, every(masks[:, TRANSPOSED + LEVELS - 1, :], GDN_H), heads(10)), "x0", c)
                    Wp("ks")
                    link(TT(heads(19), heads_of(bank(6, 2)), over(gs["beg"], P), ALU.mult))
                    ddve.done(TT(unit(9), unit(9), unit(19), ALU.subtract), "r", c)
                    for n in inv:
                        level = LEVELS - 2 - n
                        for k in range(2):
                            hs = slice(4 * k, 4 * k + 4)
                            Wp(f"x{n}{k}")
                            met()
                            if level:
                                V.copy_predicated(X[:, hs, :], every(masks[:, TRANSPOSED + level, :], 4),
                                                  heads_of(bank(4 + k)))
                            ddve.done(V.copy_predicated(Z[:, hs, :], every(masks[:, level, :], 4),
                                                        heads_of(bank(6 + k))), f"x{n}{k}", c)
                    Wp("o")
                    ddve.done(TT(heads(19), heads_of(bank(4, 2)), over(gs["rqs"], P), ALU.mult), "o1", c)
                    Wa("osq")
                    ddve.done(V.tensor_reduce(gs["oss"], heads(14), AX_X, ALU.add), "ss", c)
                    link(TT(S, S, over(gs["egl"], P), ALU.mult))
                    Wp("su")
                    ddve.done(TT(unit(15), unit(15), bank(6, 2), ALU.add), "s", c)
                    Wa("ro")
                    ddve.done(TT(heads(19), heads(19), over(gs["ro"], P), ALU.mult), "o2", c)
                    Wp("ot")
                    eng.wait_ge(loaded[3], 16 * c + 16)
                    ddve.done(STT(out=unit(19), in0=bank(2, 2), scalar=col("gdn_norm_g"), in1=unit(3), op0=ALU.mult,
                                  op1=ALU.mult), "res", c)
                    Wa("hi")
                    ddve.done(TT(act[:, :, 1, ds(c * CH, CH)], heads(19), act[:, :, 0, ds(c * CH, CH)].bitcast(F32),
                                 ALU.subtract), "lo", c)
                link.loop(NCH, 6, chunk)

            for s in (xdve, gprep, gsel, ddve):
                s.credit(eng)
            eng.sem_inc(sq_used, CREDIT)
            eng.sem_inc(mlp_acc, MLP_T)
            eng.wait_ge(const_in, 48)
            link(V.tensor_copy(masks[:], unit(14, 2).rearrange("p (m n) -> p m n", n=P)))
            sum_squares()
            eng.wait_ge(x_in, 16)
            normed("mix_pre_g", 0)
            mixer0()
            for layer in range(2):
                k0 = KT * layer
                if layer:
                    residual("mlp_post_g", 0)
                    normed("mix_pre_g", k0)
                    mixer1()
                mem_norm(layer)
                sum_squares()
                eng.wait_ge(x_in, 32)
                residual("mix_post_g", k0)
                normed("xa_pre_g", k0)
                values(layer)
                attention(layer)
                split_lo()
                sum_squares()
                residual("xa_post_g", k0)
                normed("mlp_pre_g", k0)
                mlp(layer)
                sum_squares()
            residual("mlp_post_g", KT, squares=False)

        @block.tensor
        def _(eng):
            mm, tr = nc.tensor.matmul, nc.tensor.transpose
            link = Chain(eng, None)
            count = {"square": 0, "act": 0}

            def gemm(n, n_static, u, u_static, rhs=None, kts=KT, first=0, fresh=None, width=HALF, done=True):
                w = n_static % 2
                eng.wait_ge(w_split, n + (1 + CREDIT))
                eng.wait_ge(evac, u + 1)
                out = slot(u_static)
                halves = 2 if width == HALF else 1
                rhs = rhs or (lambda kt, hl, k: act[:, kt, hl, k * HALF:(k + 1) * HALF])
                for kt in range(kts):
                    if fresh:
                        eng.wait_ge(fresh[0], fresh[1] + (kt + 1))
                    for wp, xp in ((0, 0), (0, 1), (1, 0)):
                        for k in range(halves):
                            at = first + kt * P
                            last = mm(out[:, k * HALF:k * HALF + width], whl[:, w, wp, at:at + P], rhs(kt, xp, k),
                                      start=kt == wp == xp == 0, stop=kt == kts - 1 and wp == 1)
                last.then_inc(unit_done, 1)

            def project(name, cnt, fresh=True, **kw):
                n0, u0 = plan[name]
                if fresh:
                    ready = (act_ready, KT * count["act"])
                    count["act"] += 1
                    gemm(n0, n0, u0, u0, fresh=ready, **kw)
                    gemm(n0 + 1, n0 + 1, u0 + 1, u0 + 1, **kw)
                    n0, u0, cnt = n0 + 2, u0 + 2, cnt - 2

                def body(i):
                    for j in range(2):
                        gemm(2 * i + (n0 + j), n0 + j, 2 * i + (u0 + j), u0 + j, **kw)
                link.loop(cnt // 2, 0, body)
                if cnt % 2:
                    gemm(n0 + cnt - 1, n0 + cnt - 1, u0 + cnt - 1, u0 + cnt - 1, **kw)

            def stats():
                count["square"] += 1
                eng.wait_ge(sq_used, KT * count["square"] + CREDIT)
                for k in range(2):
                    last = mm(bank(4 + k), ones, unit(SSQ)[:, k * HALF:(k + 1) * HALF], start=True, stop=True)
                last.then_inc(stat_done, 1)

            def mem_stat_():
                eng.wait_ge(mem_ssq, count.setdefault("mem", 0) + 1)
                count["mem"] += 1
                mm(bank(7)[:, 0:N_MEM], ones, small[:, 0:N_MEM], start=True, stop=True).then_inc(mem_stat, 1)

            def transposes(out, src, n):
                for h in range(n):
                    last = tr(out[:, h, :], src[:, h, :], ident)
                return last

            def value_transposes(layer, norm):
                eng.wait_ge(rstd_ready, norm)
                eng.wait_ge(evac, plan[f"xq{layer}"][1] + CREDIT)
                vt = unit(10, 2)
                for m in range(2):
                    for t in range(KT):
                        at = t * N_MEM + m * P
                        last = tr(bank(4 + 2 * m + t // 4)[:, (t % 4) * P:(t % 4 + 1) * P], vt[:, at:at + P], ident)
                last.then_inc(vt_done, 1)

            def attention(layer):
                n0, u0 = plan[f"xq{layer}"]
                q, kk = work[:, 10:12, :], unit(8, 2).rearrange("p (t m) -> p t m", m=N_MEM)
                vh = unit(SSQ)[:, 0:2 * N_MEM].rearrange("p (m d) -> p m d", m=2)
                p, pt = unit(14), unit(15)
                ready = (act_ready, KT * count["act"])
                count["act"] += 1
                gemm(n0, n0, u0, u0, fresh=ready)
                gemm(n0 + 1, n0 + 1, u0 + 1, u0 + 1)

                def head(h, more):
                    k = h + XA_H * layer

                    def scores(e):
                        for j in range(4):
                            for d in range(XA_T):
                                tok = e * HALF + j * P
                                last = mm(bank(4, 2)[:, j * N_MEM:(j + 1) * N_MEM], q[:, d, tok:tok + P],
                                          kk[:, ds(XA_T * h + d, 1), :].rearrange("p a m -> p (a m)"), start=d == 0, stop=d == 1)
                        xpe.done(last, f"S{e}")

                    def p_transposes(e):
                        eng.wait_ge(xdve.sem, xdve.at(f"N{e}", k))
                        eng.wait_ge(xdve.sem, xdve.at("O0", k) if e else xdve.at("O1", k - 1))
                        for j in range(4):
                            for m in range(2):
                                at = j * N_MEM + m * P
                                last = tr(bank(6 + m)[:, j * P:(j + 1) * P], p[:, at:at + P], ident)
                        xpe.done(last, f"T{e}")

                    def weighted(e):
                        eng.wait_ge(xact.sem, xact.at(f"P{e}", k))
                        for d in range(XA_T):
                            for m in range(2):
                                last = mm(bank(6 + d), vh[:, m, d * P:(d + 1) * P], pt[:, m * HALF:(m + 1) * HALF],
                                          start=m == 0, stop=m == 1)
                        xpe.done(last, f"V{e}")

                    def next_q(d):
                        if more:
                            gemm(2 * h + (n0 + 2 + d), n0 + d, 2 * h + (u0 + 2 + d), u0 + d)

                    eng.wait_ge(head_ready, k + 1)
                    scores(0)
                    next_q(0)
                    p_transposes(0)
                    eng.wait_ge(xact.sem, xact.at("E0", k))
                    scores(1)
                    next_q(1)
                    weighted(0)
                    p_transposes(1)
                    weighted(1)
                link.loop(XA_H - 1, 0, lambda h: head(h, True))
                head(XA_H - 1, False)

            def mlp(layer):
                n0, u0 = plan[f"mlp{layer}"]
                ready = (act_ready, KT * count["act"])
                count["act"] += 1
                per = 2 * MLP_T

                def body(g):
                    for b in range(MLP_T):
                        gemm(per * g + (n0 + b), n0 + b, U_MLP * g + (u0 + b), u0 + b, fresh=None if b else ready)
                    for b in range(MLP_T):
                        for o in range(2):
                            n, u = n0 + MLP_T + b, u0 + MLP_T + 2 * b + o
                            gemm(per * g + n, n, U_MLP * g + u, u, kts=MLP_T, first=o * MLP_T * P,
                                 rhs=lambda kt, hl, k: hid[:, kt, hl, k * HALF:(k + 1) * HALF],
                                 fresh=None if b or o else (hid_ready, MLP_T * g + MLP_T * MLP_G * layer))
                link.loop(MLP_G, 0, body)

            def mixer0():
                ua = plan["mix0a"][1]
                project("mix0a", 9)
                eng.wait_ge(lruw_in, 32)
                for t in range(LRU_T):
                    eng.wait_ge(lru_conv, t + 1)
                    for k in range(2):
                        u = ua + 9 + 2 * t + k
                        eng.wait_ge(evac, u + 1)
                        w = unit(10)[:, (4 * k + t) * P:(4 * k + t + 1) * P]
                        for half in range(2):
                            at = slice(half * HALF, (half + 1) * HALF)
                            last = mm(slot(u)[:, at], w, unit(t)[:, at], start=True, stop=True)
                        last.then_inc(unit_done, 1)
                for hp in range(2):
                    u = ua + 9 + 2 * LRU_T + hp
                    eng.wait_ge(evac, u + 1)
                    for half in range(2):
                        at = slice(half * HALF, (half + 1) * HALF)
                        last = mm(slot(u)[:, at], small[0:16, hp * P:(hp + 1) * P], unit(11)[0:16, at], start=True,
                                  stop=True)
                    last.then_inc(unit_done, 1)
                project("mix0b", 12, fresh=False)

                def chunk(c, j):
                    e, ks, q = gla["E"][j], gla["KS"][j], gla["QS"][j]
                    eng.wait_ge(gprep.sem, gprep.at("E", c))
                    eng.wait_ge(gexp.sem, gexp.at("stage", c))
                    eng.wait_ge(gev.sem, gev.at("tr", c - 1))
                    transposes(bank(4).rearrange("p (h n) -> p h n", h=4), gla["VS"][j], 4)
                    gpe.done(transposes(bank(5)[:, 0:W2].rearrange("p (h n) -> p h n", h=2), e[:, 7], 2), "tr")
                    for pair in range(4):
                        if pair < 2:
                            eng.wait_ge(gsel.sem, gsel.at(f"L{pair + 2}", c - 1))
                        else:
                            eng.wait_ge(gsel.sem, gsel.at(f"L{pair - 2}", c))
                        for lv in range(2):
                            level = 2 * pair + lv
                            for h in range(GLA_H):
                                par, hp = h % 2, h // 2
                                rows = slice(64 * par, 64 * par + 64)
                                lhs = e[rows, level, hp, :] if level < DIAG else ks[rows, hp, :]
                                rhs = e[rows, level, hp, :] if level < DIAG else q[rows, hp, :]
                                at = lv * W2 + hp * CH
                                last = mm(ps[:, 2 * (pair % 2) + par, at:at + CH], lhs, rhs, start=True, stop=True)
                        gpe.done(last, f"L{pair}")
                    eng.wait_ge(gev.sem, gev.at("tr", c))
                    eng.wait_ge(gsel.sem, gsel.at("S", c - 1))
                    eng.wait_ge(gsel.sem, gsel.at("L3", c))
                    for h in range(GLA_H):
                        par, hp = h % 2, h // 2
                        o = bank(6)[:, h * CH:(h + 1) * CH]
                        mm(o, gla["S"][:, hp, :], gla["QZ"][j][:, h, :], start=True, stop=False)
                        last = mm(o, gla["vtok"][:, h, :], gla["AT"][:, 2 * par + hp, :], start=False, stop=True)
                    gpe.done(last, "o")
                    for h in range(GLA_H):
                        par, hp = h % 2, h // 2
                        last = mm(ps[64 * par:64 * par + 64, 7, hp * P:(hp + 1) * P],
                                  gla["ktok"][:, hp, 64 * par:64 * par + 64], gla["vtok"][:, h, :], start=True,
                                  stop=True)
                    gpe.done(last, "s")

                def body(i):
                    for j in range(2):
                        chunk(2 * i + j, j)
                link.loop(NCH // 2, 0, body)
                for h in range(GLA_H):
                    eng.wait_ge(o_sq, h + 1)
                    if h >= 2:
                        eng.wait_ge(o_rstd, h - 1)
                    for half in range(2):
                        at = slice(half * HALF, (half + 1) * HALF)
                        last = mm(slot(h)[:, at], ones, unit(4 + h)[:, at], start=True, stop=True)
                    last.then_inc(o_stat, 1)

            def mixer1():
                project("mix1", 4 * GDN_H + 1)
                ub = plan["mix1"][1] + 4 * GDN_H
                eng.wait_ge(evac, ub + 1 + CREDIT)
                transposes(heads_of(bank(4, 2)), heads(7), NCH).then_inc(ba_t, 1)
                eng.wait_ge(ba_g, 1)
                mm(bank(6)[:, 0:64], tri, unit(6)[:, 512:576], start=True, stop=True).then_inc(ba_cum, 1)

                def chunk(c):
                    Wa = (lambda name: eng.wait_ge(dact.sem, dact.at(name, c)))
                    Wd = (lambda name: eng.wait_ge(ddve.sem, ddve.at(name, c)))

                    def each(first_bank, lhs, rhs, hs=range(GDN_H), start=True, stop=True):
                        for h in hs:
                            last = mm(bank(first_bank + (h // 4 - hs[0] // 4))[:, (h % 4) * P:(h % 4 + 1) * P],
                                      lhs[:, h, :], rhs[:, h, :], start=start, stop=stop)
                        return last

                    KN, KNT, R, M, AT, X, Z, Q, S, VN, KD, QG = (heads(t) for t in (7, 8, 9, 10, 11, 12, 13, 14, 15,
                                                                                 16, 17, 18))
                    Wd("dg")
                    for k in range(2):
                        last = mm(bank(k), ones, unit(4)[:, k * HALF:(k + 1) * HALF], start=True, stop=True)
                    dpe.done(last, "grow")
                    eng.wait_ge(loaded[1], 16 * c + 16)
                    dpe.done(transposes(heads_of(bank(2, 2)), heads(1), GDN_H), "kt")
                    eng.wait_ge(loaded[2], 16 * c + 16)
                    dpe.done(transposes(heads_of(bank(4, 2)), heads(2), GDN_H), "vt")
                    Wa("sqq")
                    for k, t in enumerate((19, 14)):
                        for h in range(GDN_H):
                            last = mm(bank(6)[:, 8 * k + h:8 * k + h + 1], heads(t)[:, h, :], ones[:, 0:1], start=True,
                                      stop=True)
                    dpe.done(last, "nrm")
                    Wd("kn")
                    dpe.done(transposes(heads_of(bank(2, 2)), KN, GDN_H), "knt")
                    Wa("knt")
                    dpe.done(each(6, KNT, S), "ks")
                    dpe.done(each(0, KNT, KNT), "g")
                    Wd("vb")
                    dpe.done(each(4, KNT, heads(0)), "qk")
                    Wd("x0")
                    dpe.done(transposes(heads_of(bank(2, 2)), X, GDN_H), "z")
                    for n in inv:
                        for k in range(2):
                            if n:
                                Wd(f"x{n - 1}{k}")
                            elif k == 0:
                                Wa("z")
                            dpe.done(each(k, M, Z, range(4 * k, 4 * k + 4)), f"q{n}{k}")
                        for k in range(2):
                            hs = range(4 * k, 4 * k + 4)
                            Wa(f"q{n}{k}")
                            if n == 0 and k == 0:
                                Wd("r")
                            each(4 + k, Q, X, hs)
                            dpe.done(each(6 + k, X, Q, hs), f"x{n}{k}")
                    Wd(f"x{LEVELS - 2}1")
                    dpe.done(each(0, Z, R), "vn")
                    Wa("vn")
                    for h in range(GDN_H):
                        o = bank(4 + h // 4)[:, (h % 4) * P:(h % 4 + 1) * P]
                        mm(o, QG[:, h, :], S[:, h, :], start=True, stop=False)
                        last = mm(o, AT[:, h, :], VN[:, h, :], start=False, stop=True)
                    dpe.done(last, "o")
                    dpe.done(each(6, KD, VN), "su")
                    Wd("o2")
                    dpe.done(transposes(heads_of(bank(2, 2)), heads(19), GDN_H), "ot")
                link.loop(NCH, 0, chunk)

            eng.sem_inc(unit_done, CREDIT)
            for s in (xpe, gpe, dpe):
                s.credit(eng)
            eng.wait_ge(const_in, 48)
            stats()
            mixer0()
            for layer in range(2):
                if layer:
                    stats()
                    stats()
                    mixer1()
                mem_stat_()
                if layer:
                    eng.wait_ge(ddve.sem, ddve.at("lo", NCH - 1))
                project(f"out{layer}", KT, fresh=not layer)
                stats()
                eng.wait_ge(mem_ready, layer + 1)
                project(f"kv{layer}", 2 * KT, fresh=False, width=N_MEM,
                        rhs=lambda kt, hl, k: memhl[:, hl, kt * N_MEM:(kt + 1) * N_MEM])
                stats()
                value_transposes(layer, count["square"])
                attention(layer)
                project(f"xo{layer}", KT)
                stats()
                stats()
                mlp(layer)
            stats()


def host_arrays(x):
    import numpy as np

    def block(w):
        full = np.zeros((D, P), w.dtype)
        full[:, :w.shape[1]] = w
        return full.reshape(KT, P, P).transpose(1, 0, 2).reshape(P, D)

    def blocks(w):
        return [block(w[:, n:n + P]) for n in range(0, w.shape[1], P)]

    def vector(v):
        return v.reshape(-1, P).T

    w_in, stream = x["ab_w_in"][0], []
    q, k, v, g, lr, lx, lg = np.split(w_in, [256, 512, 1024, 1536, 1552, 2064], axis=1)
    stream += blocks(lx) + blocks(lg) + blocks(lr) + blocks(v) + blocks(g) + blocks(q) + blocks(k)
    out0 = x["ab_w_out"][0]
    outs = [np.concatenate([out0[512:], out0[:512]]), x["gdn_w_out"][0]]
    for layer in range(2):
        if layer:
            w = x["gdn_w_in"][0]
            for h in range(GDN_H):
                for kind in range(4):
                    at = kind * GDN_H * P + h * P
                    stream += blocks(w[:, at:at + P])
            stream += blocks(w[:, 4 * GDN_H * P:])
        stream += blocks(outs[layer]) + blocks(x["xa_w_kv"][layer]) + blocks(x["xa_w_q"][layer])
        stream += blocks(x["xa_w_o"][layer])
        w1, w2 = x["mlp_w1"][layer], x["mlp_w2"][layer]
        for g in range(MLP_G):
            rows = slice(g * MLP_T * P, (g + 1) * MLP_T * P)
            stream += blocks(w1[:, rows])
            part = w2[rows].reshape(MLP_T, P, KT // 2, 2, P).transpose(2, 1, 3, 0, 4)
            stream += list(part.reshape(KT // 2, P, D))
    conv0 = x["lru_conv_w"][0].reshape(4, LRU_T, P).transpose(2, 1, 0).reshape(P, 16)
    conv1 = x["gdn_conv_w"][0].reshape(4, 24, P).transpose(2, 1, 0).reshape(P, 96)
    vectors = {"lru_conv_w": conv0, "gdn_conv_w": conv1,
               "gdn_dt_bias": np.repeat(x["gdn_dt_bias"], P, 0), "gdn_a_log": np.repeat(x["gdn_a_log"], P, 0)}
    pvec = np.concatenate([vectors[name] if name in vectors else vector(x[name]) for name, _ in VECTORS], axis=1)
    lru_w = np.stack([x["lru_w_a"][0], x["lru_w_x"][0]]).transpose(2, 0, 1, 3).reshape(P, D)
    tok = np.arange(P)
    consts = np.concatenate([np.eye(P), np.ones((P, P)), tok[:, None] <= tok[None, :]], axis=1).astype(np.float32)
    levels = []
    for level in range(LEVELS):
        half = P >> (level + 1)
        low, up, blk = tok // half % 2 == 0, tok // half % 2 == 1, tok // (2 * half)
        levels.append(low[:, None] & up[None, :] & (blk[:, None] == blk[None, :]))
    masks = np.stack(levels + [np.eye(P, dtype=bool)] + [m.T for m in levels] + [tok[:, None] <= tok[None, :]], axis=1)

    def tiles(a):
        return a.T.reshape(KT, P, -1).transpose(1, 0, 2)

    return {"xT": tiles(x["x"][0]), "memT": tiles(x["mem"][0]).reshape(P, KT * N_MEM), "wstream": np.stack(stream),
            "lru_w": lru_w, "gk_w2": x["gla_gk_w2"][0], "pvec_in": pvec, "consts_in": consts,
            "masks_in": masks.astype(np.float32)}


def kernel(**inputs):
    import numpy as np
    import concourse.bacc as bacc
    from concourse.bass_utils import run_bass_kernel_spmd as run

    nc = bacc.Bacc("TRN2", target_bir_lowering=False, num_devices=1)
    arrays = {k: np.ascontiguousarray(a) for k, a in host_arrays({k: np.asarray(v) for k, v in inputs.items()}).items()}
    args = {k: nc.dram_tensor(f"{k}_dram", a.shape, mybir.dt.from_np(a.dtype), kind="ExternalInput").ap()
            for k, a in arrays.items()}
    outT = nc.dram_tensor("outT_dram", (P, KT, SEQ), F32, kind="ExternalOutput").ap()
    build(nc, outT=outT, **args)
    r = run(nc, [{f"{k}_dram": a for k, a in arrays.items()}], core_ids=[0])
    got = r.results[0]["outT_dram"]
    return got.transpose(1, 0, 2).reshape(D, SEQ).T.reshape(1, SEQ, D)
```

```python
from contextlib import ExitStack

import concourse.bass as bass
from concourse import mybir

F32 = mybir.dt.float32
F32R = mybir.dt.float32r
U8 = mybir.dt.uint8
ALU = mybir.AluOpType
ACT = mybir.ActivationFunctionType
AX_X = mybir.AxisListType.X
ds = bass.ds

P = 128
D = 1024
SEQ = 1024
KT = D // P
HALF = 512
N_MEM = 256
CH = 128
NCH = SEQ // CH
LEVELS = 7
EPS = 1e-6
GLA_H, GLA_DK = 4, 64
LRU_T = 4
LRU_C = 8.0
GLA_GATE_NORM = 16.0
GDN_H = 8
XA_H = 4
XA_T = 2
MLP_G, MLP_T = 8, 4
CREDIT = 2

VECTORS = (("mix_pre_g", 16), ("mix_post_g", 16), ("xa_pre_g", 16), ("xa_mem_g", 16), ("xa_post_g", 16),
           ("mlp_pre_g", 16), ("mlp_post_g", 16), ("lru_conv_w", 16), ("lru_conv_b", 4), ("lru_b_a", 4),
           ("lru_b_x", 4), ("lru_lambda", 4), ("gla_gk_b", 2), ("gla_norm_g", 1), ("gdn_conv_w", 96),
           ("gdn_norm_g", 1), ("gdn_dt_bias", 8), ("gdn_a_log", 8))
COL = {name: sum(k for _, k in VECTORS[:n]) for n, (name, _) in enumerate(VECTORS)}
N_COL = sum(k for _, k in VECTORS)


class Steps:
    AHEAD = 2

    def __init__(self, sem, names):
        self.sem, self.names, self.next = sem, names.split(), 0

    def credit(self, eng):
        self.eng = eng
        eng.sem_inc(self.sem, self.AHEAD * len(self.names))

    def at(self, name, i=0):
        return (i + self.AHEAD) * len(self.names) + (self.names.index(name) + 1)

    def done(self, ins, name, i=None):
        assert self.names[self.next] == name, (self.names[self.next], name)
        self.next = (self.next + 1) % len(self.names)
        ins.then_inc(self.sem, 1)
        if i is not None:
            self.eng.wait_ge(self.sem, self.at(name, i))


class Chain:

    def __init__(self, eng, sem):
        self.eng, self.sem, self.base, self.k = eng, sem, 0, 0

    def __call__(self, ins):
        ins.then_inc(self.sem, 1)
        self.k += 1
        self.eng.wait_ge(self.sem, self.base + self.k)

    def loop(self, n, per, body):
        base, self.k = self.base + self.k, 0
        with self.eng.Fori(0, n) as i:
            self.base = i * per + base if per else base
            body(i)
            assert self.k == per, (self.k, per)
        self.base, self.k = base + n * per, 0


def schedule():
    plan, after = {}, []
    unit = 0

    def stage(name, blocks, extra=0):
        nonlocal unit
        plan[name] = (len(after), unit)
        for _ in range(blocks):
            unit += 1
            after.append(unit)
        unit += extra

    stage("mix0a", 9, extra=2 * LRU_T + 2)
    stage("mix0b", 12)
    for layer in range(2):
        if layer:
            stage("mix1", 4 * GDN_H + 1)
        stage(f"out{layer}", KT)
        stage(f"kv{layer}", 2 * KT)
        stage(f"xq{layer}", KT)
        stage(f"xo{layer}", KT)
        plan[f"mlp{layer}"] = (len(after), unit)
        for _ in range(MLP_G):
            for b in range(2 * MLP_T):
                unit += 1 + b // MLP_T
                after.append(unit)
    return plan, after


def build(nc, xT, memT, wstream, lru_w, gk_w2, pvec_in, consts_in, masks_in, outT):
    plan, after = schedule()
    NB = len(after)
    U_MLP = 3 * MLP_T
    base = (nc.sbuf_base + 63) // 64 * 64

    with ExitStack() as ctx:
        def place(name, kib, shape, dt):
            return nc.alloc_sbuf_tensor_at(name, shape, dt, offset=base + int(kib * 1024))

        def sem(name):
            return ctx.enter_context(nc.semaphore(name))

        hres = place("hres", 0, [P, KT, SEQ], F32)
        lin = place("lin", 0, [P, KT * SEQ], F32)
        act = place("act", 32, [P, KT, 2, SEQ], F32R)
        wraw = place("wraw", 96, [P, 2, D], F32)
        whl = place("whl", 104, [P, 2, 2, D], F32R)
        consts = place("consts", 120, [P, 3 * P], F32)
        masks = place("masks", 121.5, [P, 2 * LEVELS + 2, P], U8)
        pvec = place("pvec", 123.5, [P, N_COL + 2], F32)
        small = place("small", 124.75, [P, 320], F32)
        work = place("work", 126, [P, 20, SEQ], F32)
        hid = place("hid", 126 + 8 * 4, [P, MLP_T, 2, SEQ], F32R)
        memhl = place("memhl", 126 + 12 * 4, [P, 2, KT * N_MEM], F32R)
        ps = ctx.enter_context(nc.psum_tensor("ps", [P, 8, HALF], F32))
        qkvz = nc.dram_tensor("qkvz", [4, GDN_H, P, SEQ], F32, kind="Internal").ap()

        ident, ones, tri = consts[:, 0:P], consts[:, P:2 * P], consts[:, 2 * P:3 * P]
        one_col, eps_col = pvec[:, N_COL:N_COL + 1], pvec[:, N_COL + 1:N_COL + 2]
        DIAG, TRANSPOSED, CAUSAL = LEVELS, LEVELS + 1, 2 * LEVELS + 1

        def flat(ap):
            return ap.rearrange("p a n -> p (a n)")

        def unit(t, n=1):
            return flat(work[:, t:t + n, :])

        def heads(t, n=GDN_H):
            return unit(t)[:, 0:n * P].rearrange("p (h n) -> p h n", h=n)

        def heads_of(ap):
            return ap.rearrange("p (h n) -> p h n", n=P)

        def tile(buf, t):
            return flat(buf[:, ds(t, 1), :])

        def part(t, hl):
            return act[:, ds(t, 1), hl, :].rearrange("p a n -> p (a n)")

        def bank(b, n=1):
            return flat(ps[:, b:b + n, :])

        def slot(u):
            return bank(2 * (u % 2), 2)

        def col(name, k=0):
            return pvec[:, ds(k + COL[name], 1)]

        def over(ap, n):
            return ap.unsqueeze(2).to_broadcast([P, ap.shape[1], n])

        def every(ap, n):
            return ap.unsqueeze(1).to_broadcast([P, n, ap.shape[1]])

        SQ, SSQ, RSTD = 16, 18, 19

        w_in = [sem("w_in0"), sem("w_in1")]
        w_hi = sem("w_hi")
        w_hi_act = [sem("w_hi_act0"), sem("w_hi_act1")]
        w_split = sem("w_split")
        unit_done = sem("unit_done")
        evac = sem("evac")
        const_in, mask_in, x_in, m_in, lruw_in = (sem(f"{k}_in") for k in ("const", "mask", "x", "m", "lruw"))
        x_tile_in = [sem(f"x_tile{t}_in") for t in range(KT)]
        cols_set = sem("cols_set")
        act_chain, dve_chain = sem("act_chain"), sem("dve_chain")
        act_waits, dve_waits = sem("act_waits"), sem("dve_waits")
        sq_done, sq_used = sem("sq_done"), sem("sq_used")
        stat_done, rstd_ready = sem("stat_done"), sem("rstd_ready")
        xn_ready = sem("xn_ready")
        hi_ready, act_ready = sem("hi_ready"), sem("act_ready")
        h_new = sem("h_new")
        mem_sq, mem_ssq, mem_stat, mem_rstd = sem("mem_sq"), sem("mem_ssq"), sem("mem_stat"), sem("mem_rstd")
        mem_n, mem_hi, mem_ready = sem("mem_n"), sem("mem_hi"), sem("mem_ready")
        vt_done, v_ready = sem("vt_done"), sem("v_ready")
        head_ready = sem("head_ready")
        first_scores = sem("first_scores")
        xpe = Steps(sem("xa_pe"), "T0 S1 V0 T1 V1")
        xact = Steps(sem("xa_act"), "E0 P0 E1 P1")
        xdve = Steps(sem("xa_dve"), "M0 N0 M1 O0 N1 O1")
        mlp_scaled, hid_hi, hid_ready = sem("mlp_scaled"), sem("hid_hi"), sem("hid_ready")
        gate_ready = sem("gate_ready")
        lru_conv, lru_lam, lru_in = sem("lru_conv"), sem("lru_lam"), sem("lru_in")
        lam_exp, lru_decay, lru_gain, lru_root, lru_y = (sem("lam_exp"), sem("lru_decay"), sem("lru_gain"),
                                                         sem("lru_root"), sem("lru_y"))
        gk_log, gk_part, gk_cum = sem("gk_log"), sem("gk_part"), sem("gk_cum")
        gprep = Steps(sem("gla_prep"), "sub")
        gpool = Steps(sem("gla_pool"), "E")
        gsel = Steps(sem("gla_select"), "m0 L0 m1 L1 m2 L2 m3 L3 S")
        gexp = Steps(sem("gla_exp"), "exp stage")
        gev = Steps(sem("gla_evac"), "tr o")
        gpe = Steps(sem("gla_pe"), "tr L0 L1 L2 L3 o s")
        o_sq, o_stat, o_ln, o_rstd, o_n = (sem(f"o_{k}") for k in ("sq", "stat", "ln", "rstd", "n"))
        conv_done, silu_done = sem("conv_done"), sem("silu_done")
        z_used = sem("z_used")
        stored = [sem("stored0"), sem("stored1")]
        loaded = [sem(f"loaded_{k}") for k in "qkvz"]
        ba_t, ba_copy, ba_sig, ba_x, ba_exp, ba_g, ba_cum, ba_done = (
            sem("ba_t"), sem("ba_copy"), sem("ba_sig"), sem("ba_x"), sem("ba_exp"), sem("ba_g"), sem("ba_cum"),
            sem("ba_done"))
        inv = range(LEVELS - 1)
        ppe = Steps(sem("gdn_prep_pe"), "grow kt nrm knt vt g qk z " +
                    " ".join(f"q{n}0 q{n}1 x{n}0 x{n}1" for n in inv))
        fpe = Steps(sem("gdn_fin_pe"), "ks vn o su ot")
        pact = Steps(sem("gdn_prep_act"), "sqk sqq rk eg L LT sc knt z " + " ".join(f"q{n}0 q{n}1" for n in inv))
        fact = Steps(sem("gdn_fin_act"), "vn osq ro hi")
        ppool = Steps(sem("gdn_prep_pool"), "L qg kd")
        pdve = Steps(sem("gdn_prep_dve"), "dg m kn vb mn x0 beg at " +
                     " ".join(f"z{n}{k} x{n}{k}" for n in inv for k in range(2) if n < LEVELS - 2) +
                     f" z{LEVELS - 2}0 z{LEVELS - 2}1")
        fdve = Steps(sem("gdn_fin_dve"), "r o1 s ss o2 res lo")
        out_done = sem("out_done")

        def in_lin(first, *shape):
            n = 1
            for k in shape:
                n *= k
            names = "abc"[:len(shape)]
            return lin[:, first:first + n].rearrange(f"p ({' '.join(names)}) -> p {' '.join(names)}",
                                                     **dict(zip(names, shape)))

        W2, W4 = 2 * CH, 4 * CH
        gla = {
            "E": [in_lin(j * 9 * W2, 9, 2, CH) for j in range(2)],
            "QZ": [in_lin(18 * W2 + j * W4, 4, CH) for j in range(2)],
            "AT": in_lin(18 * W2 + 2 * W4, 4, CH),
            "ktok": in_lin(18 * W2 + 3 * W4, 2, CH),
            "vtok": in_lin(19 * W2 + 3 * W4, 4, CH),
            "S": in_lin(19 * W2 + 4 * W4, 2, P),
            "VS": [in_lin(20 * W2 + (4 + j) * W4, 4, CH) for j in range(2)],
            "KS": [unit(18)[:, j * W2:(j + 1) * W2].rearrange("p (h n) -> p h n", h=2) for j in range(2)],
            "QS": [unit(18)[:, (2 + j) * W2:(3 + j) * W2].rearrange("p (h n) -> p h n", h=2) for j in range(2)],
            "decay": [small[:, 308 + 2 * j:310 + 2 * j].unsqueeze(2) for j in range(2)],
        }
        gs = {name: small[:, 128 + 8 * k:128 + 8 * k + n] for name, k, n in
              (("rkq", 0, 16), ("dec", 2, 8), ("gd", 3, 8), ("egl", 4, 8), ("gl", 5, 8), ("egt", 6, 8), ("g", 7, 8),
               ("ro", 8, 8), ("oss", 9, 8), ("nb", 10, 8), ("bt", 11, 8), ("beg", 12, 8), ("rqs", 13, 8), ("egs", 14, 8))}

        def halves(ap, level):
            half = CH >> (level + 1)
            v = ap.rearrange("p h (n s t) -> p h n s t", s=2, t=half)
            return v[:, :, :, 0, :], v[:, :, :, 1, :]

        def gdn_chunks(link, prepare, finish, both, per):
            prepare(0)
            link.loop(NCH - 2, per, lambda c: both(c, True))
            both(NCH - 2, False)
            finish(NCH - 1)

        def chunks(link, prepare, finish, per):
            prepare(0, 0)

            def body(i):
                for j in range(2):
                    prepare(2 * i + (j + 1), 1 - j)
                    finish(2 * i + j, j)
            link.loop(NCH // 2 - 1, per, body)
            prepare(NCH - 1, 1)
            finish(NCH - 2, 0)
            finish(NCH - 1, 1)

        block = ctx.enter_context(nc.Block())

        @block.sync
        def _(sp):
            sp.dma_start(consts[:], consts_in).then_inc(const_in, 16)
            sp.dma_start(pvec[:, 0:N_COL], pvec_in).then_inc(const_in, 16)
            with sp.Fori(0, NB // 2) as i:
                for j in range(2):
                    sp.wait_ge(w_split, 2 * i + (j + 1))
                    sp.dma_start(wraw[:, j, :], wstream[ds(2 * i + j, 1), :, :].rearrange("b p n -> (b p) n")) \
                        .then_inc(w_in[j], 16)
            for n in range(NB // 2 * 2, NB):
                sp.wait_ge(w_split, n + 1)
                sp.dma_start(wraw[:, n % 2, :], wstream[n]).then_inc(w_in[n % 2], 16)
            sp.wait_ge(out_done, 16 * KT)

        @block.gpsimd
        def _(pool):
            def split(n, arrived, hi_n, used):
                j = n % 2
                pool.wait_ge(unit_done, used)
                pool.wait_ge(w_in[j], arrived)
                nc.gpsimd.tensor_tensor(whl[:, j, 0, :], wraw[:, j, :], one_col.to_broadcast([P, D]),
                                        ALU.mult).then_inc(w_hi, 1)
                pool.wait_ge(w_hi, hi_n)
                nc.gpsimd.tensor_tensor(whl[:, j, 1, :], wraw[:, j, :], whl[:, j, 0, :].bitcast(F32),
                                        ALU.subtract).then_inc(w_split, 1)

            def one(n):
                split(n, 16 * (n // 2 + 1), n + 1, (after[n - 2] if n >= 2 else n - 1) + CREDIT)

            def sum_squares(norm):
                n0 = KT * norm
                pool.wait_ge(rstd_ready, norm)
                nc.gpsimd.memset(unit(SSQ), 0.0).then_inc(cols_set, 1)
                sets[0] += 1
                pool.wait_ge(cols_set, 2 + sets[0])
                for t in range(KT):
                    pool.wait_ge(sq_done, n0 + t + 1)
                    nc.gpsimd.tensor_tensor(unit(SSQ), unit(SSQ), unit(SQ + t % 2), ALU.add).then_inc(sq_used, 1)
                    pool.wait_ge(sq_used, n0 + t + 1 + CREDIT)

            sets = [0]

            def run(n0, cnt, between=None):
                one(n0)
                one(n0 + 1)
                if between:
                    between()
                with pool.Fori(0, (cnt - 2) // 2) as i:
                    for n in (n0 + 2, n0 + 3):
                        split(n, 16 * i + 16 * (n // 2 + 1), 2 * i + (n + 1), 2 * i + (after[n - 2] + CREDIT))
                for n in range(n0 + cnt // 2 * 2, n0 + cnt):
                    one(n)

            def run_lo(n0, cnt, layer):
                with pool.Fori(0, cnt // 2) as i:
                    for n in (n0, n0 + 1):
                        pool.wait_ge(w_hi_act[n % 2], i + (cnt // 2 * layer + 1))
                        nc.gpsimd.tensor_tensor(whl[:, n % 2, 1, :], wraw[:, n % 2, :],
                                                whl[:, n % 2, 0, :].bitcast(F32), ALU.subtract).then_inc(w_split, 1)
                pool.sem_inc(w_hi, cnt)

            def mlp(n0, between):
                per = 2 * MLP_T
                for n in range(n0, n0 + per):
                    one(n)
                    if n == n0 + 1:
                        between()
                with pool.Fori(0, MLP_G - 1) as g:
                    for n in range(n0 + per, n0 + 2 * per):
                        split(n, 8 * per * g + 16 * (n // 2 + 1), per * g + (n + 1),
                              U_MLP * g + (after[n - 2] + CREDIT))

            def gla_prepare(c, j):
                tt = nc.gpsimd.tensor_tensor
                e, b = gla["E"][j], work[:, 16:18, ds(c * CH, CH)]
                pool.wait_ge(gpe.sem, gpe.at("o", c - 2))
                for level in range(LEVELS):
                    b_lo, b_up = halves(b, level)
                    e_lo, e_up = halves(e[:, level], level)
                    ref = b_lo[:, :, :, b_lo.shape[3] - 1:b_lo.shape[3]].to_broadcast(list(b_lo.shape))
                    tt(e_lo, ref, b_lo, ALU.subtract)
                    tt(e_up, b_up, ref, ALU.subtract)
                gprep.done(tt(e[:, 7], b[:, :, CH - 1:CH].to_broadcast([P, 2, CH]), b, ALU.subtract), "sub")
                q, k = (work[:, t:t + 2, ds(c * CH, CH)] for t in (4, 6))
                pool.wait_ge(gexp.sem, gexp.at("exp", c))
                if isinstance(c, int):
                    pool.wait_ge(evac, plan["mix0b"][1] + 12 + CREDIT)
                for level in range(LEVELS):
                    e_lo, e_up = halves(e[:, level], level)
                    tt(e_lo, e_lo, halves(k, level)[0], ALU.mult)
                    tt(e_up, e_up, halves(q, level)[1], ALU.mult)
                gpool.done(tt(e[:, 7], e[:, 7], k, ALU.mult), "E")

            def gdn(p):
                pool.wait_ge(pact.sem, pact.at("L", p))
                ppool.done(nc.gpsimd.tensor_tensor(heads(5), heads(5), over(gs["nb"], CH), ALU.mult), "L")
                pool.wait_ge(fpe.sem, fpe.at("su", p - 1))
                ppool.done(nc.gpsimd.tensor_tensor(unit(18), unit(4), unit(0), ALU.mult), "qg")
                pool.wait_ge(pact.sem, pact.at("sc", p))
                pool.wait_ge(pdve.sem, pdve.at("kn", p))
                ppool.done(nc.gpsimd.tensor_tensor(heads(17), heads(7), over(gs["dec"], P), ALU.mult), "kd")

            pool.sem_inc(w_split, CREDIT)
            ppool.credit(pool)
            gpool.credit(pool)
            gprep.credit(pool)
            nc.gpsimd.memset(one_col, 1.0).then_inc(cols_set, 1)
            nc.gpsimd.memset(eps_col, EPS).then_inc(cols_set, 1)
            pool.wait_ge(cols_set, 2)
            run(plan["mix0a"][0], 9)
            run(plan["mix0b"][0], 12)
            pool.wait_ge(gk_cum, 2 * NCH)
            pool.wait_ge(lru_y, LRU_T)
            for j in range(2):
                gla_prepare(j, j)
            with pool.Fori(1, NCH // 2) as i:
                for j in range(2):
                    gla_prepare(2 * i + j, j)
            for layer in range(2):
                if layer:
                    run(plan["mix1"][0], 4 * GDN_H + 1, between=lambda: sum_squares(6))
                    with pool.Fori(0, NCH) as p:
                        gdn(p)
                run(plan[f"out{layer}"][0], KT)
                one(plan[f"kv{layer}"][0])
                one(plan[f"kv{layer}"][0] + 1)
                run_lo(plan[f"kv{layer}"][0] + 2, 2 * KT, layer)
                run(plan[f"xq{layer}"][0] + 2, 2 * KT - 2)
                mlp(plan[f"mlp{layer}"][0], between=lambda: sum_squares(4 + 6 * layer))

        @block.scalar
        def _(eng):
            A = nc.scalar.activation
            link = Chain(eng, act_chain)
            count = {"square": 0, "hi": 0, "norm": 0}

            def met():
                eng.sem_inc(act_waits, 1)

            def square(src, n0, i, j):
                eng.wait_ge(sq_used, 2 * i + (n0 + j + 1))
                met()
                A(unit(SQ + j), src, ACT.Square).then_inc(sq_done, 1)

            def squares_from(src, ready):
                n0 = KT * count["square"]
                count["square"] += 1

                def body(i):
                    for j in range(2):
                        eng.wait_ge(ready[0], 2 * i + (ready[1] + j + 1))
                        square(src(2 * i + j), n0, i, j)
                link.loop(KT // 2, 0, body)

            def rstd():
                count["norm"] += 1
                link(A(small[:, 319:320], one_col, ACT.Ln))
                eng.wait_ge(stat_done, count["norm"])
                link(A(unit(RSTD), bank(4, 2), ACT.Ln, scale=1.0 / D, bias=eps_col))
                A(unit(RSTD), unit(RSTD), ACT.Exp, scale=-0.5).then_inc(rstd_ready, 1)

            def evacuate(u, u_static, out, func=ACT.Copy, **kw):
                eng.wait_ge(unit_done, u + (1 + CREDIT))
                return A(out, slot(u_static), func, **kw).then_inc(evac, 1)

            def out_epilogue(u0, between=None):
                n0 = KT * count["square"]
                count["square"] += 1

                def body(i):
                    for j in range(2):
                        eng.wait_ge(unit_done, 2 * i + (u0 + j + 1 + CREDIT))
                        square(slot(u0 + j), n0, i, j)
                        A(tile(work, 2 * i + j), slot(u0 + j), ACT.Copy).then_inc(evac, 1)
                link.loop(KT // 4, 0, body)
                if between:
                    between()
                link.loop(KT // 4, 0, lambda i: body(i + KT // 4))

            def mem_norm(layer):
                eng.dma_start(unit(8, 2), memT).then_inc(m_in, 16)
                eng.wait_ge(m_in, 16 * (layer + 1))
                A(unit(10, 2), unit(8, 2), ACT.Square).then_inc(mem_sq, 1)

            def mem_norm_end(layer):
                eng.wait_ge(mem_stat, layer + 1)
                link(A(small[:, 0:N_MEM], bank(7)[:, 0:N_MEM], ACT.Ln, scale=1.0 / D, bias=eps_col))
                A(small[:, 0:N_MEM], small[:, 0:N_MEM], ACT.Exp, scale=-0.5).then_inc(mem_rstd, 1)
                eng.wait_ge(mem_n, layer + 1)
                A(memhl[:, 0, :], unit(8, 2), ACT.Copy).then_inc(mem_hi, 1)

            def first_parts():
                count["square"] += 1
                count["hi"] += 1
                for t in range(KT):
                    eng.wait_ge(x_tile_in[t], 16)
                    A(part(t, 0), tile(hres, t), ACT.Copy, scale=col("mix_pre_g", t)).then_inc(hi_ready, 1)
                    square(tile(hres, t), 0, t // 2, t % 2)

            def parts_of_residual(gain, k0, h0):
                n0 = KT * count["square"]
                count["square"] += 1

                def body(i):
                    for j in range(2):
                        residual_parts(gain, k0, h0, n0, i, j)
                link.loop(KT // 2, 0, body)

            def residual_parts(gain, k0, h0, n0, i, j):
                h = tile(hres, 2 * i + j)
                eng.wait_ge(h_new, 2 * i + (h0 + j + 1))
                met()
                A(part(2 * i + j, 0), h, ACT.Copy, scale=col(gain, 2 * i + (k0 + j))).then_inc(hi_ready, 1)
                square(h, n0, i, j)

            def residual_and_kv(layer, h0):
                b0, u0 = plan[f"kv{layer}"]
                n0 = KT * count["square"]
                count["square"] += 1
                kv = unit(8, 4).rearrange("p (t m) -> p t m", m=N_MEM)
                eng.wait_ge(mem_ready, layer + 1)

                def body(i):
                    for j in range(2):
                        for k in (2 * j, 2 * j + 1):
                            eng.wait_ge(unit_done, 4 * i + (u0 + k + 1 + CREDIT))
                            met()
                            A(flat(kv[:, ds(4 * i + k, 1), :]), slot(u0 + k)[:, 0:N_MEM], ACT.Copy) \
                                .then_inc(evac, 1)
                            n = b0 + k + 2
                            eng.wait_ge(w_in[n % 2], 32 * i + 16 * (n // 2 + 1))
                            A(whl[:, n % 2, 0, :], wraw[:, n % 2, :], ACT.Copy).then_inc(w_hi_act[n % 2], 1)
                        residual_parts("xa_pre_g", KT * layer, h0, n0, i, j)
                link.loop(KT // 2, 0, body)

            def attention(layer):
                vh = unit(SSQ)[:, 0:2 * N_MEM].rearrange("p (m d) -> p m d", m=2)
                v = work[:, 12:14, :]
                p, pt = unit(14), unit(15)
                mx, den = small[:, 256:264], small[:, 264:272]
                eng.wait_ge(v_ready, 4 * (layer + 1))

                def body(h):
                    k = h + XA_H * layer
                    eng.wait_ge(xpe.sem, xpe.at("V1", k - 1))
                    A(vh, v[:, :, ds(h * N_MEM, N_MEM)], ACT.Copy).then_inc(head_ready, 1)
                    for e in range(2):
                        eng.wait_ge(xdve.sem, xdve.at(f"M{e}", k))
                        eng.wait_ge(xpe.sem, xpe.at("T0", k) if e else xpe.at("T1", k - 1))
                        for j in range(4):
                            at = slice(j * N_MEM, (j + 1) * N_MEM)
                            last = A(p[:, at], bank(4, 2)[:, at], ACT.Exp, bias=mx[:, 4 * e + j:4 * e + j + 1],
                                     accum_out=den[:, 4 * e + j:4 * e + j + 1])
                        xact.done(last, f"E{e}", k)
                        eng.wait_ge(xpe.sem, xpe.at(f"T{e}", k))
                        xact.done(A(pt, bank(6, 2), ACT.Copy), f"P{e}", k)
                link.loop(XA_H, 0, body)

            def split_hi(layer):
                count["hi"] += 1
                eng.wait_ge(xdve.sem, xdve.at("O1", XA_H * (layer + 1) - 1))

                def body(i):
                    for j in range(2):
                        A(part(2 * i + j, 0), tile(work, 2 * i + j), ACT.Copy).then_inc(hi_ready, 1)
                link.loop(KT // 2, 0, body)

            def mlp(layer):
                u0 = plan[f"mlp{layer}"][1]

                def body(g):
                    h0 = MLP_T * MLP_G * layer
                    for t in range(MLP_T):
                        eng.wait_ge(hid_ready, MLP_T * g + (h0 + t + 1))
                        if t == 0:
                            eng.wait_ge(evac, U_MLP * g + (u0 + CREDIT))
                        evacuate(U_MLP * g + (u0 + t), u0 + t, unit(SQ + t % 2), ACT.Relu)
                        eng.wait_ge(mlp_scaled, MLP_T * g + (h0 + t + 1))
                        link(A(unit(SQ + t % 2), unit(SQ + t % 2), ACT.Square))
                        A(hid[:, t, 0, :], unit(SQ + t % 2), ACT.Copy).then_inc(hid_hi, 1)
                link.loop(MLP_G, MLP_T, body)

            def store_tile(i, j, h0):
                eng.wait_ge(h_new, 2 * i + (h0 + j + 1))
                eng.dma_start(outT[:, ds(2 * i + j, 1), :].rearrange("p a n -> p (a n)"),
                              tile(hres, 2 * i + j)).then_inc(out_done, 16)

            def mixer0():
                ua, ub = plan["mix0a"][1], plan["mix0b"][1]
                R, I = (lambda t: lin[:, t * SEQ:(t + 1) * SEQ]), (lambda t: lin[:, (4 + t) * SEQ:(5 + t) * SEQ])
                for t in range(LRU_T):
                    eng.wait_ge(evac, ua + 4 + t + 1 + CREDIT)
                    A(unit(4 + t), unit(4 + t), ACT.Gelu_apprx_tanh).then_inc(gate_ready, 1)
                eng.wait_ge(evac, ua + 9 + CREDIT)
                for t in range(LRU_T):
                    u = ua + 9 + 2 * t
                    evacuate(u, u, R(t), ACT.Sigmoid, bias=col("lru_b_a", t))
                    evacuate(u + 1, u + 1, I(t), ACT.Sigmoid, bias=col("lru_b_x", t))
                for hp in range(2):
                    u, gk = ua + 9 + 2 * LRU_T + hp, unit(16 + hp)
                    evacuate(u, u, gk, ACT.Identity, bias=col("gla_gk_b", hp))
                    eng.wait_ge(evac, u + 1 + CREDIT)
                    if hp:
                        eng.wait_ge(gk_part, 1)
                    link(A(unit(18), gk, ACT.Abs))
                    link(A(unit(18), unit(18), ACT.Exp, scale=-1.0))
                    A(unit(18), unit(18), ACT.Ln, bias=one_col).then_inc(gk_log, 1)
                eng.wait_ge(lru_lam, 1)
                for t in range(LRU_T):
                    eng.wait_ge(lru_in, t + 1)
                    A(unit(t), R(t), ACT.Exp, scale=small[:, 300 + t:301 + t])
                    A(R(t), R(t), ACT.Tanh, scale=small[:, 304 + t:305 + t]).then_inc(lru_decay, 1)
                for t in range(LRU_T):
                    eng.wait_ge(lru_gain, t + 1)
                    A(R(t), R(t), ACT.Sqrt).then_inc(lru_root, 1)
                for t in range(GLA_H):
                    eng.wait_ge(evac, ub + 4 + t + 1 + CREDIT)
                    A(unit(12 + t), unit(12 + t), ACT.Silu).then_inc(gate_ready, 1)
                eng.wait_ge(lru_y, LRU_T)

                def prepare(c, j):
                    e, vs, ks = gla["E"][j], gla["VS"][j], gla["KS"][j]
                    eng.wait_ge(gpe.sem, gpe.at("L3", c - 2))
                    eng.wait_ge(gprep.sem, gprep.at("sub", c))
                    eng.wait_ge(gsel.sem, gsel.at("S", c - 2))
                    A(e[:, 0:8], e[:, 0:8], ACT.Exp)
                    A(e[:, 8], work[:, 16:18, ds(c * CH, CH)], ACT.Exp)
                    gexp.done(A(gla["decay"][j], work[:, 16:18, ds(c * CH + (CH - 1), 1)], ACT.Exp), "exp", c)
                    if isinstance(c, int) and c == 0:
                        eng.wait_ge(evac, ub + 12 + CREDIT)
                    met()
                    A(vs, work[:, 8:12, ds(c * CH, CH)], ACT.Copy)
                    A(gla["QS"][j], work[:, 4:6, ds(c * CH, CH)], ACT.Copy)
                    gexp.done(A(ks, work[:, 6:8, ds(c * CH, CH)], ACT.Copy), "stage", c)

                def finish(c, j):
                    eng.wait_ge(gpe.sem, gpe.at("tr", c))
                    A(gla["ktok"], bank(5)[:, 0:2 * P].rearrange("p (h n) -> p h n", h=2), ACT.Copy)
                    gev.done(A(gla["vtok"], bank(4).rearrange("p (h n) -> p h n", h=4), ACT.Copy), "tr", c)
                    eng.wait_ge(gpe.sem, gpe.at("o", c))
                    met()
                    gev.done(A(work[:, 8:12, ds(c * CH, CH)], bank(6).rearrange("p (h n) -> p h n", h=4), ACT.Copy),
                             "o", c)

                count["hi"] += 1
                chunks(link, prepare, finish, 0)
                eng.wait_ge(gsel.sem, gsel.at("S", NCH - 1))
                eng.dma_start(hres[:], xT).then_inc(x_in, 16)
                eng.wait_ge(gev.sem, gev.at("o", NCH - 1))
                for h in range(GLA_H):
                    A(unit(4 + h), unit(8 + h), ACT.Square).then_inc(o_sq, 1)
                for h in range(GLA_H):
                    eng.wait_ge(o_stat, h + 1)
                    A(unit(4 + h), bank(4 + 2 * (h % 2), 2), ACT.Ln, scale=1.0 / P, bias=eps_col).then_inc(o_ln, 1)
                eng.wait_ge(o_ln, GLA_H)
                for h in range(GLA_H):
                    A(unit(4 + h), unit(4 + h), ACT.Exp, scale=-0.5).then_inc(o_rstd, 1)
                eng.wait_ge(act_ready, KT + LRU_T)
                for h in range(GLA_H):
                    eng.wait_ge(o_n, h + 1)
                    A(part(LRU_T + h, 0), unit(8 + h), ACT.Copy).then_inc(hi_ready, 1)
                eng.wait_ge(act_ready, 2 * KT)

            def mixer1():
                u0 = plan["mix1"][1]
                eng.sem_inc(stored[0], 16)
                eng.sem_inc(stored[1], 16)
                eng.sem_inc(silu_done, 3)
                eng.sem_inc(z_used, 1)

                def store(kind, h, s):
                    eng.dma_start(qkvz[kind, ds(h, 1), :, :].rearrange("h p n -> (h p) n"),
                                  unit(2 + s)).then_inc(stored[s], 16)

                def body(h):
                    def silu(k, s, nth):
                        eng.wait_ge(conv_done, 3 * h + (k + 1))
                        eng.wait_ge(stored[s], 32 * h + (16 * nth + 16))
                        A(unit(2 + s), unit(4 + k), ACT.Silu).then_inc(silu_done, 1)
                        eng.wait_ge(silu_done, 3 * h + (k + 1 + 3))
                        store(k, h, s)

                    silu(0, 0, 0)
                    silu(1, 1, 0)
                    silu(2, 1, 1)
                    eng.wait_ge(stored[0], 32 * h + 32)
                    eng.wait_ge(evac, 4 * h + (u0 + 5 + CREDIT))
                    A(unit(2), unit(8), ACT.Silu).then_inc(z_used, 1)
                    eng.wait_ge(z_used, h + 2)
                    store(3, h, 0)
                body(0)
                eng.wait_ge(ba_copy, 1)
                beta = small[:, 64:128].rearrange("p (c h) -> p c h", c=NCH)
                ba = unit(9)[:, 0:128].rearrange("p (c k) -> p c k", c=NCH)
                A(beta, ba[:, :, 0:GDN_H], ACT.Sigmoid).then_inc(ba_sig, 1)
                eng.wait_ge(ba_x, 1)
                A(unit(9)[:, 192:256], unit(9)[:, 128:192], ACT.Abs).then_inc(ba_sig, 1)
                eng.wait_ge(ba_sig, 2)
                A(unit(9)[:, 192:256], unit(9)[:, 192:256], ACT.Exp, scale=-1.0)
                A(unit(9)[:, 256:264], pvec[:, COL["gdn_a_log"]:COL["gdn_a_log"] + 8], ACT.Exp).then_inc(ba_exp, 1)
                body(1)
                link.loop(GDN_H - 2, 0, lambda h: body(h + 2))
                def in_dram(kind):
                    done = 16 + 32 * GDN_H
                    eng.wait_ge(stored[kind in (1, 2)], done - 16 if kind in (0, 1) else done)

                def load(kind, c):
                    eng.dma_start(heads(kind), qkvz[kind, :, :, ds(c * CH, CH)].rearrange("h p n -> p h n")) \
                        .then_inc(loaded[kind], 16)

                def loads(p):
                    eng.wait_ge(pdve.sem, pdve.at("at", p - 1))
                    eng.wait_ge(ppool.sem, ppool.at("kd", p - 1))
                    for kind in (1, 0, 2):
                        load(kind, p)

                def squares(p):
                    eng.wait_ge(ppe.sem, ppe.at(f"x{LEVELS - 2}1", p - 1))
                    eng.wait_ge(pdve.sem, pdve.at("dg", p))
                    eng.wait_ge(loaded[1], 16 * p + 16)
                    pact.done(A(unit(7), unit(1), ACT.Square), "sqk", p)
                    eng.wait_ge(loaded[0], 16 * p + 16)
                    pact.done(A(unit(14), unit(0), ACT.Square), "sqq", p)
                    eng.wait_ge(ppe.sem, ppe.at("nrm", p))
                    link(A(gs["rkq"], bank(4)[:, 0:16], ACT.Ln, bias=eps_col))
                    pact.done(A(gs["rkq"], gs["rkq"], ACT.Exp, scale=-0.5), "rk", p)

                def new_values(c):
                    eng.wait_ge(fpe.sem, fpe.at("vn", c))
                    fact.done(A(unit(16), bank(6, 2), ACT.Copy), "vn", c)

                def decays(p):
                    eng.wait_ge(pdve.sem, pdve.at("m", p))
                    pact.done(A(unit(4), bank(0, 2), ACT.Exp), "eg", p)
                    pact.done(A(unit(5), unit(5), ACT.Exp), "L", p)
                    pact.done(A(unit(6), unit(6), ACT.Exp, scale=-1.0), "LT", p)
                    A(gs["dec"], gs["gd"], ACT.Exp)
                    A(gs["egl"], gs["gl"], ACT.Exp)
                    pact.done(A(gs["egt"], gs["g"], ACT.Exp), "sc", p)
                    eng.wait_ge(ppe.sem, ppe.at("knt", p))
                    pact.done(A(unit(8), bank(2, 2), ACT.Copy), "knt", p)

                def output_squares(c):
                    eng.wait_ge(fdve.sem, fdve.at("o1", c))
                    eng.wait_ge(fpe.sem, fpe.at("su", c))
                    fact.done(A(unit(16), unit(19), ACT.Square), "osq", c)

                def output_rms(c):
                    eng.wait_ge(fdve.sem, fdve.at("ss", c))
                    link(A(gs["ro"], gs["oss"], ACT.Ln, scale=1.0 / P, bias=eps_col))
                    fact.done(A(gs["ro"], gs["ro"], ACT.Exp, scale=-0.5), "ro", c)

                def first_z(p):
                    eng.wait_ge(ppe.sem, ppe.at("z", p))
                    pact.done(A(unit(13), bank(0, 2), ACT.Copy), "z", p)

                def level(p, n):
                    for g in range(2):
                        eng.wait_ge(ppe.sem, ppe.at(f"q{n}{g}", p))
                        pact.done(A(unit(14)[:, g * HALF:(g + 1) * HALF], bank(g), ACT.Copy), f"q{n}{g}", p)

                def result_hi(c):
                    eng.wait_ge(fdve.sem, fdve.at("res", c))
                    met()
                    fact.done(A(act[:, :, 0, ds(c * CH, CH)], heads(19), ACT.Copy), "hi", c)

                def prepare(p):
                    for kind in (1, 0, 2):
                        in_dram(kind)
                        load(kind, p)
                    squares(p)
                    decays(p)
                    first_z(p)
                    for n in inv:
                        level(p, n)
                        if n == 0:
                            loads(p + 1)
                    in_dram(3)

                def both(c, more):
                    load(3, c)
                    squares(c + 1)
                    new_values(c)
                    decays(c + 1)
                    output_squares(c)
                    first_z(c + 1)
                    for n in inv:
                        level(c + 1, n)
                        if n == 0:
                            output_rms(c)
                            if more:
                                loads(c + 2)
                        if n == 3:
                            result_hi(c)

                def finish(c):
                    load(3, c)
                    new_values(c)
                    output_squares(c)
                    output_rms(c)
                    result_hi(c)

                gdn_chunks(link, prepare, finish, both, 2)

            eng.sem_inc(evac, CREDIT)
            for s in (xact, gexp, gev, pact, fact):
                s.credit(eng)
            for t in range(KT):
                eng.dma_start(hres[:, t, :], xT[:, t, :]).then_inc(x_tile_in[t], 16)
            eng.dma_start(unit(10), lru_w).then_inc(lruw_in, 16)
            eng.dma_start(small[0:16, 0:256], gk_w2).then_inc(lruw_in, 16)
            eng.dma_start(unit(14, 2), masks_in.rearrange("p m n -> p (m n)")).then_inc(mask_in, 16)
            eng.wait_ge(const_in, 32)
            eng.wait_ge(cols_set, 2)
            first_parts()
            link(A(small[:, 284:288], pvec[:, COL["lru_lambda"]:COL["lru_lambda"] + 4], ACT.Abs))
            A(small[:, 284:288], small[:, 284:288], ACT.Exp, scale=-1.0).then_inc(lam_exp, 1)
            rstd()
            mixer0()
            for layer in range(2):
                h0 = 3 * KT * layer
                if layer:
                    rstd()
                    parts_of_residual("mix_pre_g", KT, 2 * KT)
                    rstd()
                    mixer1()
                mem_norm(layer)
                out_epilogue(plan[f"out{layer}"][1], between=lambda: mem_norm_end(layer))
                rstd()
                residual_and_kv(layer, h0)
                rstd()
                attention(layer)
                split_hi(layer)
                out_epilogue(plan[f"xo{layer}"][1])
                rstd()
                parts_of_residual("mlp_pre_g", KT * layer, h0 + KT)
                rstd()
                mlp(layer)
                squares_from(lambda t: tile(work, t),
                             (evac, plan[f"mlp{layer}"][1] + U_MLP * (MLP_G - 1) + MLP_T + CREDIT))
            rstd()
            link.loop(KT // 2, 0, lambda i: [store_tile(i, j, 5 * KT) for j in range(2)])

        @block.vector
        def _(eng):
            V = nc.vector
            TT, TS, STT = V.tensor_tensor, V.tensor_scalar, V.scalar_tensor_tensor
            link = Chain(eng, dve_chain)
            count = {"square": 0, "hi": 0, "norm": 0}

            def met():
                eng.sem_inc(dve_waits, 1)

            def add_square(n0, i, j):
                eng.wait_ge(sq_done, 2 * i + (n0 + j + 1))
                eng.wait_ge(sq_used, 2 * i + (n0 + j + CREDIT))
                TT(unit(SSQ), unit(SSQ), unit(SQ + j), ALU.add).then_inc(sq_used, 1)

            def sum_squares(between=None):
                n0 = KT * count["square"]
                count["square"] += 1
                link(V.memset(unit(SSQ), 0.0))

                def body(i):
                    for j in range(2):
                        add_square(n0, i, j)
                link.loop(KT // 4, 0, body)
                if between:
                    between()
                link.loop(KT // 4, 0, lambda i: body(i + KT // 4))

            def wait_rstd():
                count["norm"] += 1
                eng.wait_ge(rstd_ready, count["norm"])

            def residual(gain, k0, squares=True):
                wait_rstd()
                n0 = KT * count["square"]
                if squares:
                    count["square"] += 1
                    link(V.memset(unit(SSQ), 0.0))

                def body(i):
                    for j in range(2):
                        m = tile(work, 2 * i + j)
                        link(STT(out=m, in0=m, scalar=col(gain, 2 * i + (k0 + j)), in1=unit(RSTD), op0=ALU.mult,
                                 op1=ALU.mult))
                    for j in range(2):
                        h = tile(hres, 2 * i + j)
                        TT(h, h, tile(work, 2 * i + j), ALU.add).then_inc(h_new, 1)
                    if squares:
                        for j in range(2):
                            add_square(n0, i, j)
                link.loop(KT // 2, 2, body)

            def residual_and_lo(gain, k0, pre_gain, pre_k0, add=False):
                wait_rstd()
                n0, nh = KT * count["square"], KT * count["hi"]
                count["square"] += 1
                count["hi"] += 1
                if add:
                    link(V.memset(unit(SSQ), 0.0))

                def normed(i, t):
                    m = tile(work, 2 * i + t)
                    link(STT(out=m, in0=m, scalar=col(gain, 2 * i + (k0 + t)), in1=unit(RSTD), op0=ALU.mult,
                             op1=ALU.mult))

                def added(i, t):
                    h = tile(hres, 2 * i + t)
                    TT(h, h, tile(work, 2 * i + t), ALU.add).then_inc(h_new, 1)

                def lo(i, t):
                    eng.wait_ge(hi_ready, 2 * i + (nh + t + 1))
                    STT(out=part(2 * i + t, 1), in0=tile(hres, 2 * i + t), scalar=col(pre_gain, 2 * i + (pre_k0 + t)),
                        in1=part(2 * i + t, 0).bitcast(F32), op0=ALU.mult, op1=ALU.subtract).then_inc(act_ready, 1)
                    if add:
                        add_square(n0, i + t // 2, t % 2)

                def body(i):
                    for t in (2, 3):
                        normed(i, t)
                        added(i, t)
                        lo(i, t - 1)

                normed(0, 0)
                added(0, 0)
                normed(0, 1)
                lo(0, 0)
                added(0, 1)
                link.loop(KT // 2 - 1, 2, body)
                lo(0, KT - 1)

            def lo_part(t, src, n0, i, j):
                eng.wait_ge(hi_ready, 2 * i + (n0 + j + 1))
                TT(part(t, 1), src, part(t, 0).bitcast(F32), ALU.subtract).then_inc(act_ready, 1)
                eng.wait_ge(act_ready, 2 * i + (n0 + j + 1))

            def first_lo():
                count["square"] += 1
                count["hi"] += 1
                link(V.memset(unit(SSQ), 0.0))
                for t in range(KT):
                    eng.wait_ge(hi_ready, t + 1)
                    STT(out=part(t, 1), in0=tile(hres, t), scalar=col("mix_pre_g", t), in1=part(t, 0).bitcast(F32),
                        op0=ALU.mult, op1=ALU.subtract).then_inc(act_ready, 1)
                    add_square(0, t // 2, t % 2)

            def convolve(x, out, w, bias, done):
                if bias is None:
                    link(TS(out, x, w(3), None, ALU.mult))
                else:
                    link(TS(out, x, w(3), bias, ALU.mult, ALU.add))
                for back in (1, 2, 3):
                    ins = STT(out=out[:, back:], in0=x[:, 0:SEQ - back], scalar=w(3 - back), in1=out[:, back:],
                              op0=ALU.mult, op1=ALU.add)
                    if back < 3:
                        link(ins)
                ins.then_inc(done, 1)

            def log1p(e, out, s, s2):
                link(TS(s, e, 2.0, None, ALU.add))
                link(V.reciprocal(s, s))
                link(TT(s, s, e, ALU.mult))
                link(TT(s2, s, s, ALU.mult))
                link(TS(out, s2, 1.0 / 17, None, ALU.mult))
                for k in range(15, 1, -2):
                    link(STT(out=out, in0=out, scalar=1.0 / k, in1=s2, op0=ALU.add, op1=ALU.mult))
                link(STT(out=out, in0=out, scalar=1.0, in1=s, op0=ALU.add, op1=ALU.mult))
                link(TS(out, out, 2.0, None, ALU.mult))

            def mem_norm(layer):
                eng.wait_ge(mem_sq, layer + 1)
                V.tensor_reduce(small[:, 0:N_MEM], unit(10, 2).rearrange("p (k m) -> p m k", k=KT), AX_X,
                                ALU.add).then_inc(mem_ssq, 1)

            def mem_norm_end(layer):
                eng.wait_ge(mem_rstd, layer + 1)
                for k in range(KT):
                    m = unit(8, 2)[:, k * N_MEM:(k + 1) * N_MEM]
                    last = STT(out=m, in0=m, scalar=col("xa_mem_g", KT * layer + k), in1=small[:, 0:N_MEM],
                               op0=ALU.mult, op1=ALU.mult)
                last.then_inc(mem_n, 1)
                eng.wait_ge(mem_hi, layer + 1)
                TT(memhl[:, 1, :], unit(8, 2), memhl[:, 0, :].bitcast(F32), ALU.subtract).then_inc(mem_ready, 1)

            def values(layer):
                eng.wait_ge(vt_done, layer + 1)
                for m in range(2):
                    for k in range(2):
                        V.tensor_copy(unit(12 + m)[:, k * HALF:(k + 1) * HALF], bank(4 + 2 * m + k)) \
                            .then_inc(v_ready, 1)

            def attention(layer):
                mx, den, rd = small[:, 256:264], small[:, 264:272], small[:, 272:280]
                u0, qh = plan[f"xq{layer}"][1], work[:, 10:12, :]
                s4 = bank(4, 2).rearrange("p (t m) -> p t m", t=4)
                p4 = unit(14).rearrange("p (t m) -> p t m", t=4)

                def queries(h, d):
                    eng.wait_ge(unit_done, XA_T * h + (u0 + d + 1 + CREDIT))
                    STT(out=qh[:, d, :], in0=slot(u0 + d), scalar=float(XA_T * P) ** -0.5, in1=unit(RSTD),
                        op0=ALU.mult, op1=ALU.mult).then_inc(evac, 1)

                def head(h, more):
                    k = h + XA_H * layer

                    def maxima(e):
                        if e:
                            eng.wait_ge(xpe.sem, xpe.at("S1", k))
                        else:
                            eng.wait_ge(first_scores, k + 1)
                        m = mx[:, 4 * e:4 * e + 4]
                        link(V.tensor_reduce(m, s4, AX_X, ALU.max))
                        xdve.done(TS(m, m, -1.0, None, ALU.mult), f"M{e}", k)

                    def normalise(e):
                        eng.wait_ge(xact.sem, xact.at(f"E{e}", k))
                        r = rd[:, 4 * e:4 * e + 4]
                        link(V.reciprocal(r, den[:, 4 * e:4 * e + 4]))
                        xdve.done(TT(p4, p4, over(r, N_MEM), ALU.mult), f"N{e}", k)

                    def output(e):
                        eng.wait_ge(xpe.sem, xpe.at(f"V{e}", k))
                        xdve.done(V.tensor_copy(work[:, ds(XA_T * h, XA_T), e * HALF:(e + 1) * HALF], ps[:, 6:8, :]),
                                  f"O{e}", k)

                    maxima(0)
                    normalise(0)
                    maxima(1)
                    if more:
                        queries(h + 1, 0)
                    output(0)
                    normalise(1)
                    if more:
                        queries(h + 1, 1)
                    output(1)

                for d in range(XA_T):
                    queries(0, d)
                link.loop(XA_H - 1, 4, lambda h: head(h, True))
                head(XA_H - 1, False)

            def split_lo():
                n0 = KT * count["hi"]
                count["hi"] += 1

                def body(i):
                    for j in range(2):
                        lo_part(2 * i + j, tile(work, 2 * i + j), n0, i, j)
                link.loop(KT // 2, 0, body)

            def mlp(layer):
                u0 = plan[f"mlp{layer}"][1]
                h0 = MLP_T * MLP_G * layer
                link(V.memset(work[:, 0:8, :], 0.0))
                wait_rstd()
                n0 = KT * count["square"]
                count["square"] += 1

                def body(g, last=False):
                    for t in range(MLP_T):
                        buf = unit(SQ + t % 2)
                        eng.wait_ge(evac, U_MLP * g + (u0 + t + 1 + CREDIT))
                        TT(buf, buf, unit(RSTD), ALU.mult).then_inc(mlp_scaled, 1)
                        eng.wait_ge(hid_hi, MLP_T * g + (h0 + t + 1))
                        TT(hid[:, t, 1, :], buf, hid[:, t, 0, :].bitcast(F32), ALU.subtract).then_inc(hid_ready, 1)
                    eng.wait_ge(evac, U_MLP * g + (u0 + MLP_T + CREDIT))
                    for t in range(2 * MLP_T):
                        eng.wait_ge(unit_done, U_MLP * g + (u0 + MLP_T + t + 1 + CREDIT))
                        TT(unit(t), unit(t), slot(u0 + MLP_T + t), ALU.add).then_inc(evac, 1)
                        if last and t:
                            add_square(n0, (t - 1) // 2, (t - 1) % 2)
                link.loop(MLP_G - 1, 0, body)
                link(V.memset(unit(SSQ), 0.0))
                body(MLP_G - 1, last=True)
                add_square(n0, KT // 2 - 1, 1)

            def decay_rates():
                lam = pvec[:, COL["lru_lambda"]:COL["lru_lambda"] + 4]
                eng.wait_ge(lam_exp, 1)
                log1p(small[:, 284:288], small[:, 288:292], small[:, 292:296], small[:, 296:300])
                link(TS(small[:, 292:296], lam, -1.0, 0.0, ALU.mult, ALU.max))
                link(TT(small[:, 288:292], small[:, 288:292], small[:, 292:296], ALU.add))
                TS(small[:, 300:304], small[:, 288:292], -LRU_C, None, ALU.mult)
                TS(small[:, 304:308], small[:, 288:292], LRU_C, None, ALU.mult).then_inc(lru_lam, 1)

            def mixer0():
                ua = plan["mix0a"][1]
                R, I = (lambda t: lin[:, t * SEQ:(t + 1) * SEQ]), (lambda t: lin[:, (4 + t) * SEQ:(5 + t) * SEQ])
                wait_rstd()
                ub = plan["mix0b"][1]

                def scaled(u, out, factor=1.0):
                    eng.wait_ge(unit_done, u + 1 + CREDIT)
                    STT(out=out, in0=slot(u), scalar=factor, in1=unit(RSTD), op0=ALU.mult, op1=ALU.mult) \
                        .then_inc(evac, 1)

                for t in range(LRU_T):
                    scaled(ua + t, unit(8 + t % 2))
                    eng.wait_ge(evac, ua + t + 1 + CREDIT)
                    convolve(unit(8 + t % 2), unit(t), lambda k: col("lru_conv_w", 4 * t + k), col("lru_conv_b", t),
                             lru_conv)
                    eng.wait_ge(lru_conv, t + 1)
                for t in range(LRU_T):
                    scaled(ua + 4 + t, unit(4 + t))
                scaled(ua + 8, unit(11))
                for t in range(LRU_T):
                    eng.wait_ge(evac, ua + 9 + 2 * t + 2 + CREDIT)
                    TT(I(t), I(t), unit(t), ALU.mult).then_inc(lru_in, 1)

                def gla_gate(hp):
                    gk = unit(16 + hp)
                    eng.wait_ge(gk_log, hp + 1)
                    link(TS(gk, gk, 0.0, 1.0 / GLA_GATE_NORM, ALU.min, ALU.mult))
                    STT(out=gk, in0=unit(18), scalar=-1.0 / GLA_GATE_NORM, in1=gk, op0=ALU.mult, op1=ALU.add) \
                        .then_inc(gk_part, 1)
                    eng.wait_ge(gk_part, hp + 1)

                    def scan(c):
                        b = gk[:, ds(c * CH, CH)]
                        V.tensor_tensor_scan(b, ones, b, 0.0, ALU.mult, ALU.add).then_inc(gk_cum, 1)
                    link.loop(NCH, 0, scan)

                def lru_gains(t):
                    eng.wait_ge(lru_decay, t + 1)
                    link(TT(unit(18), unit(t), unit(t), ALU.mult))
                    STT(out=R(t), in0=unit(18), scalar=1.0, in1=R(t), op0=ALU.add, op1=ALU.mult) \
                        .then_inc(lru_gain, 1)
                    eng.wait_ge(lru_gain, t + 1)

                def lru_scan(t):
                    eng.wait_ge(lru_root, t + 1)
                    link(TT(I(t), I(t), R(t), ALU.mult))
                    link(V.tensor_tensor_scan(R(t), unit(t), I(t), 0.0, ALU.mult, ALU.add))
                    eng.wait_ge(gate_ready, t + 1)
                    TT(unit(t), R(t), unit(4 + t), ALU.mult).then_inc(lru_y, 1)

                eng.wait_ge(evac, ub + CREDIT)
                scaled(ub, unit(8))
                gla_gate(0)
                scaled(ub + 1, unit(9))
                gla_gate(1)
                for t in (2, 3):
                    scaled(ub + t, unit(8 + t))
                    lru_gains(2 * t - 4)
                    lru_gains(2 * t - 3)
                for t in range(GLA_H):
                    scaled(ub + 4 + t, unit(12 + t))
                    lru_scan(t)
                eng.wait_ge(lru_y, LRU_T)
                for buf in (*gla["QZ"], gla["AT"], gla["S"]):
                    link(V.memset(buf, 0.0))
                for t in range(2):
                    scaled(ub + 8 + t, unit(4 + t), float(GLA_DK) ** -0.5)
                for t in range(2):
                    scaled(ub + 10 + t, unit(6 + t))
                eng.wait_ge(gk_cum, 2 * NCH)
                eng.wait_ge(evac, plan["mix0b"][1] + 12 + CREDIT)
                n0 = KT * count["hi"]
                count["hi"] += 1

                def finish(c, j):
                    at4 = gla["AT"].rearrange("p (a b) n -> p a b n", a=2)
                    qz = gla["QZ"][j].rearrange("p (h r) n -> p h r n", r=2)
                    eng.wait_ge(gexp.sem, gexp.at("exp", c))
                    for par in range(2):
                        rows = slice(64 * par, 64 * par + 64)
                        TT(qz[rows, :, par, :], gla["E"][j][rows, 8], work[rows, 4:6, ds(c * CH, CH)], ALU.mult)
                    eng.wait_ge(gpe.sem, gpe.at("o", c - 1))
                    for pair in range(4):
                        eng.wait_ge(gpe.sem, gpe.at(f"L{pair}", c))
                        met()
                        for lv in range(2):
                            mask = masks[:, 2 * pair + lv, :].unsqueeze(1).unsqueeze(1).to_broadcast([P, 2, 2, CH])
                            data = ps[:, 2 * (pair % 2):2 * (pair % 2) + 2, lv * W2:(lv + 1) * W2] \
                                .rearrange("p a (b n) -> p a b n", b=2)
                            gsel.done(V.copy_predicated(at4, mask, data), f"L{pair}" if lv else f"m{pair}", c)
                            if not lv:
                                met()
                    eng.wait_ge(gpe.sem, gpe.at("s", c))
                    eng.wait_ge(gsel.sem, gsel.at("S", c - 1))
                    for hp in range(2):
                        s = gla["S"][:, hp, :]
                        last = STT(out=s, in0=s, scalar=gla["decay"][j][:, hp, :], in1=bank(7)[:, hp * P:(hp + 1) * P],
                                   op0=ALU.mult, op1=ALU.add)
                    gsel.done(last, "S", c)

                link.loop(NCH // 2, 0, lambda i: [finish(2 * i + j, j) for j in range(2)])
                for t in range(LRU_T):
                    V.tensor_copy(part(t, 0), unit(t)).then_inc(hi_ready, 1)
                    eng.wait_ge(hi_ready, n0 + t + 1)
                    TT(part(t, 1), unit(t), part(t, 0).bitcast(F32), ALU.subtract).then_inc(act_ready, 1)
                for h in range(GLA_H):
                    eng.wait_ge(o_rstd, h + 1)
                    o = unit(8 + h)
                    link(STT(out=o, in0=o, scalar=col("gla_norm_g"), in1=unit(4 + h), op0=ALU.mult, op1=ALU.mult))
                    eng.wait_ge(gate_ready, LRU_T + h + 1)
                    TT(o, o, unit(12 + h), ALU.mult).then_inc(o_n, 1)
                for h in range(GLA_H):
                    eng.wait_ge(hi_ready, n0 + LRU_T + h + 1)
                    TT(part(LRU_T + h, 1), unit(8 + h), part(LRU_T + h, 0).bitcast(F32), ALU.subtract) \
                        .then_inc(act_ready, 1)

            def mixer1():
                u0 = plan["mix1"][1]

                wait_rstd()

                def scaled(u, u_static, out):
                    eng.wait_ge(unit_done, u + (1 + CREDIT))
                    TT(out, slot(u_static), unit(RSTD), ALU.mult).then_inc(evac, 1)

                def body(h):
                    for k in range(4):
                        if k == 3:
                            eng.wait_ge(z_used, h + 1)
                            scaled(4 * h + (u0 + 4), u0 + 4, unit(8))
                            continue
                        scaled(4 * h + (u0 + 1 + k), u0 + 1 + k, unit(k % 2))
                        eng.wait_ge(evac, 4 * h + (u0 + k + 2 + CREDIT))
                        eng.wait_ge(silu_done, 3 * h + (k + 1))
                        convolve(unit(k % 2), unit(4 + k), lambda tap: col("gdn_conv_w", 4 * h + (32 * k + tap)),
                                 None, conv_done)
                        eng.wait_ge(conv_done, 3 * h + (k + 1))
                scaled(u0, u0, unit(7))
                body(0)
                grids = unit(9)

                def grid(first, n=8):
                    return grids[:, first:first + NCH * n].rearrange("p (c k) -> p c k", c=NCH)

                eng.wait_ge(ba_t, 1)
                V.tensor_copy(grid(0, 16), heads_of(bank(4, 2))[:, :, 0:16]).then_inc(ba_copy, 1)
                eng.wait_ge(ba_copy, 1)
                dt = pvec[:, COL["gdn_dt_bias"]:COL["gdn_dt_bias"] + 8]
                TT(grid(128), grid(0, 16)[:, :, 8:16], every(dt, NCH), ALU.add).then_inc(ba_x, 1)
                body(1)
                eng.wait_ge(ba_exp, 1)
                log1p(grids[:, 192:256], grids[:, 320:384], grids[:, 384:448], grids[:, 448:512])
                link(TS(grids[:, 128:192], grids[:, 128:192], 0.0, None, ALU.max))
                link(TT(grids[:, 320:384], grids[:, 320:384], grids[:, 128:192], ALU.add))
                link(TT(grid(320), grid(320), every(grids[:, 256:264], NCH), ALU.mult))
                TS(grids[:, 512:576], grids[:, 320:384], -1.0, None, ALU.mult).then_inc(ba_g, 1)
                link.loop(GDN_H - 2, 9, lambda h: body(h + 2))
                eng.wait_ge(silu_done, 3 * GDN_H + 3)
                eng.wait_ge(ba_cum, 1)
                link(V.tensor_copy(small[:, 0:64], bank(6)[:, 0:64]))
                link(V.memset(unit(15), 0.0))
                eng.wait_ge(ba_sig, 2)

                def on_pe(steps, name, i):
                    eng.wait_ge(steps.sem, steps.at(name, i))

                on_act = on_pool = on_pe
                g, L, LT, S = heads(4), heads(5), heads(6), heads(15)
                X, Z = heads(12), heads(13)

                def start(p):
                    on_pool(ppool, "kd", p - 1)
                    V.tensor_copy(gs["egs"], gs["egl"])
                    TS(gs["rqs"], gs["rkq"][:, 8:16], float(P) ** -0.5, None, ALU.mult)
                    V.tensor_copy(gs["g"], small[:, ds(p * GDN_H, GDN_H)])
                    link(V.tensor_copy(gs["bt"], small[:, ds(p * GDN_H + 64, GDN_H)]))
                    TS(gs["nb"], gs["bt"], -1.0, None, ALU.mult)
                    pdve.done(TT(g, every(ident, GDN_H), over(gs["g"], CH), ALU.mult), "dg", p)

                def rhs(c):
                    on_pe(fpe, "ks", c)
                    link(TT(heads(19), heads_of(bank(6, 2)), over(gs["beg"], P), ALU.mult))
                    fdve.done(TT(unit(9), unit(9), unit(19), ALU.subtract), "r", c)

                def differences(p):
                    on_pe(ppe, "grow", p)
                    grow = heads_of(bank(0, 2))
                    V.tensor_copy(gs["gl"], grow[:, :, CH - 1:CH].rearrange("p h o -> p (h o)"))
                    link(TT(g, over(gs["g"], CH), grow, ALU.subtract))
                    TT(gs["gd"], gs["gl"], gs["g"], ALU.subtract)
                    TS(unit(5), unit(4), 0.0, None, ALU.min)
                    pdve.done(TS(unit(6), unit(4), 0.0, None, ALU.max), "m", p)

                def keys(p):
                    on_pe(ppe, "kt", p)
                    on_act(pact, "rk", p)
                    pdve.done(TT(heads(7), heads_of(bank(2, 2)), over(gs["rkq"][:, 0:8], P), ALU.mult), "kn", p)

                def values_(p):
                    on_pe(ppe, "vt", p)
                    pdve.done(TT(heads(9), heads_of(bank(4, 2)), over(gs["bt"], P), ALU.mult), "vb", p)

                def output_state(c, su_bank=0):
                    on_pe(fpe, "o", c)
                    fdve.done(TT(heads(19), heads_of(bank(6, 2)), over(gs["rqs"], P), ALU.mult), "o1", c)
                    link(TT(S, S, over(gs["egs"], P), ALU.mult))
                    on_pe(fpe, "su", c)
                    fdve.done(TT(unit(15), unit(15), bank(su_bank, 2), ALU.add), "s", c)

                def identity(p):
                    link(V.tensor_copy(X, every(ident, GDN_H)))

                def decayed(p):
                    on_act(pact, "sc", p)
                    pdve.done(TT(gs["beg"], gs["bt"], gs["egt"], ALU.mult), "beg", p)
                    link(TT(LT, LT, every(masks[:, CAUSAL, :], GDN_H), ALU.mult))

                def output_squares(c):
                    on_act(fact, "osq", c)
                    fdve.done(V.tensor_reduce(gs["oss"], heads(16), AX_X, ALU.add), "ss", c)

                def matrix(p):
                    on_pool(ppool, "L", p)
                    on_pe(ppe, "g", p)
                    pdve.done(TT(unit(10), bank(6, 2), unit(5), ALU.mult), "mn", p)
                    met()
                    pdve.done(V.copy_predicated(X, every(masks[:, TRANSPOSED + LEVELS - 1, :], GDN_H), heads(10)),
                              "x0", p)

                def scores(p):
                    on_pe(ppe, "qk", p)
                    pdve.done(TT(unit(11), bank(4, 2), unit(6), ALU.mult), "at", p)

                def output_scaled(c):
                    on_act(fact, "ro", c)
                    fdve.done(TT(heads(19), heads(19), over(gs["ro"], P), ALU.mult), "o2", c)

                def level(p, n):
                    lv = LEVELS - 2 - n
                    for k in range(2):
                        hs = slice(4 * k, 4 * k + 4)
                        on_pe(ppe, f"x{n}{k}", p)
                        met()
                        pdve.done(V.copy_predicated(Z[:, hs, :], every(masks[:, lv, :], 4), heads_of(bank(6 + k))),
                                  f"z{n}{k}")
                        if lv:
                            pdve.done(V.copy_predicated(X[:, hs, :], every(masks[:, TRANSPOSED + lv, :], 4),
                                                        heads_of(bank(4 + k))), f"x{n}{k}")

                def result(c, ot_bank=2):
                    on_pe(fpe, "ot", c)
                    eng.wait_ge(loaded[3], 16 * c + 16)
                    fdve.done(STT(out=unit(19), in0=bank(ot_bank, 2), scalar=col("gdn_norm_g"), in1=unit(3), op0=ALU.mult,
                                  op1=ALU.mult), "res", c)

                def result_lo(c):
                    on_act(fact, "hi", c)
                    fdve.done(TT(act[:, :, 1, ds(c * CH, CH)], heads(19), act[:, :, 0, ds(c * CH, CH)].bitcast(F32),
                                 ALU.subtract), "lo", c)

                def prepare(p):
                    start(p)
                    identity(p)
                    differences(p)
                    keys(p)
                    values_(p)
                    matrix(p)
                    decayed(p)
                    scores(p)
                    for n in inv:
                        level(p, n)

                def both(c, more):
                    p = c + 1
                    start(p)
                    identity(p)
                    rhs(c)
                    differences(p)
                    keys(p)
                    values_(p)
                    output_state(c)
                    matrix(p)
                    output_squares(c)
                    decayed(p)
                    scores(p)
                    for n in inv:
                        level(p, n)
                        if n == 0:
                            output_scaled(c)
                        if n == 2:
                            result(c)
                        if n == 4:
                            result_lo(c)

                def finish(c):
                    link(V.tensor_copy(gs["egs"], gs["egl"]))
                    link(TS(gs["rqs"], gs["rkq"][:, 8:16], float(P) ** -0.5, None, ALU.mult))
                    rhs(c)
                    output_state(c, su_bank=4)
                    output_squares(c)
                    output_scaled(c)
                    result(c, ot_bank=4)
                    result_lo(c)

                for name in ("egl", "rkq"):
                    link(V.memset(gs[name], 0.0))
                gdn_chunks(link, prepare, finish, both, 6)

            for s in (xdve, gsel, pdve, fdve):
                s.credit(eng)
            eng.sem_inc(sq_used, CREDIT)
            eng.sem_inc(hid_ready, CREDIT)
            eng.wait_ge(const_in, 32)
            first_lo()
            eng.wait_ge(mask_in, 16)
            link(V.tensor_copy(masks[:], unit(14, 2).rearrange("p (m n) -> p m n", n=P)))
            decay_rates()
            mixer0()
            for layer in range(2):
                k0 = KT * layer
                if layer:
                    residual_and_lo("mlp_post_g", 0, "mix_pre_g", k0)
                    mixer1()
                mem_norm(layer)
                sum_squares(between=lambda: mem_norm_end(layer))
                eng.wait_ge(x_in, 16)
                residual_and_lo("mix_post_g", k0, "xa_pre_g", k0, add=True)
                wait_rstd()
                values(layer)
                attention(layer)
                split_lo()
                sum_squares()
                residual_and_lo("xa_post_g", k0, "mlp_pre_g", k0)
                mlp(layer)
            residual("mlp_post_g", KT, squares=False)

        @block.tensor
        def _(eng):
            mm, tr = nc.tensor.matmul, nc.tensor.transpose
            link = Chain(eng, None)
            count = {"square": 0, "act": 0}

            def gemm(n, n_static, u, u_static, rhs=None, kts=KT, first=0, fresh=None, width=HALF, done=True):
                w = n_static % 2
                eng.wait_ge(w_split, n + (1 + CREDIT))
                eng.wait_ge(evac, u + 1)
                out = slot(u_static)
                halves = 2 if width == HALF else 1
                rhs = rhs or (lambda kt, hl, k: act[:, kt, hl, k * HALF:(k + 1) * HALF])
                for kt in range(kts):
                    if fresh:
                        eng.wait_ge(fresh[0], fresh[1] + (kt + 1))
                    for wp, xp in ((0, 0), (0, 1), (1, 0)):
                        for k in range(halves):
                            at = first + kt * P
                            last = mm(out[:, k * HALF:k * HALF + width], whl[:, w, wp, at:at + P], rhs(kt, xp, k),
                                      start=kt == wp == xp == 0, stop=kt == kts - 1 and wp == 1)
                last.then_inc(unit_done, 1)

            def fresh_pair(n, u, ready):
                eng.wait_ge(w_split, n + 2 + CREDIT)
                eng.wait_ge(evac, u + 1)
                for kt in range(KT):
                    eng.wait_ge(ready[0], ready[1] + kt + 1)
                    for j in range(2):
                        if kt == 0 and j:
                            eng.wait_ge(evac, u + 2)
                        for wp, xp in ((0, 0), (0, 1), (1, 0)):
                            for k in range(2):
                                last = mm(slot(u + j)[:, k * HALF:(k + 1) * HALF],
                                          whl[:, (n + j) % 2, wp, kt * P:(kt + 1) * P],
                                          act[:, kt, xp, k * HALF:(k + 1) * HALF], start=kt == wp == xp == 0,
                                          stop=kt == KT - 1 and wp == 1)
                        if kt == KT - 1:
                            last.then_inc(unit_done, 1)

            def hidden_pair(n, n_static, u, u_static, ready):
                eng.wait_ge(w_split, n + (1 + CREDIT))
                eng.wait_ge(evac, u + 1)
                for kt in range(MLP_T):
                    eng.wait_ge(ready[0], ready[1] + (kt + 1))
                    for j in range(2):
                        if kt == 0 and j:
                            eng.wait_ge(evac, u + 2)
                        at = (j * MLP_T + kt) * P
                        for wp, xp in ((0, 0), (0, 1), (1, 0)):
                            for k in range(2):
                                last = mm(slot(u_static + j)[:, k * HALF:(k + 1) * HALF],
                                          whl[:, n_static % 2, wp, at:at + P], hid[:, kt, xp, k * HALF:(k + 1) * HALF],
                                          start=kt == wp == xp == 0, stop=kt == MLP_T - 1 and wp == 1)
                        if kt == MLP_T - 1:
                            last.then_inc(unit_done, 1)

            def project(name, cnt, fresh=True, between=None, after_units=2, **kw):
                n0, u0 = plan[name]
                if between and not fresh:
                    n0, u0, cnt = n0 + 2, u0 + 2, cnt - 2
                if fresh:
                    ready = (act_ready, KT * count["act"])
                    count["act"] += 1
                    fresh_pair(n0, u0, ready)
                    n0, u0, cnt = n0 + 2, u0 + 2, cnt - 2
                if between:
                    for k in range(after_units - 2):
                        gemm(n0 + k, n0 + k, u0 + k, u0 + k, **kw)
                    between()
                    n0, u0, cnt = n0 + after_units - 2, u0 + after_units - 2, cnt - (after_units - 2)

                def body(i):
                    for j in range(2):
                        gemm(2 * i + (n0 + j), n0 + j, 2 * i + (u0 + j), u0 + j, **kw)
                link.loop(cnt // 2, 0, body)
                if cnt % 2:
                    gemm(n0 + cnt - 1, n0 + cnt - 1, u0 + cnt - 1, u0 + cnt - 1, **kw)

            def stats():
                count["square"] += 1
                eng.wait_ge(sq_used, KT * count["square"] + CREDIT)
                for k in range(2):
                    last = mm(bank(4 + k), ones, unit(SSQ)[:, k * HALF:(k + 1) * HALF], start=True, stop=True)
                last.then_inc(stat_done, 1)

            def mem_stat_():
                eng.wait_ge(mem_ssq, count.setdefault("mem", 0) + 1)
                count["mem"] += 1
                mm(bank(7)[:, 0:N_MEM], ones, small[:, 0:N_MEM], start=True, stop=True).then_inc(mem_stat, 1)

            def transposes(out, src, n):
                for h in range(n):
                    last = tr(out[:, h, :], src[:, h, :], ident)
                return last

            def value_transposes(layer, norm):
                eng.wait_ge(rstd_ready, norm)
                eng.wait_ge(evac, plan[f"xq{layer}"][1] + CREDIT)
                vt = unit(10, 2)
                for m in range(2):
                    for t in range(KT):
                        at = t * N_MEM + m * P
                        last = tr(bank(4 + 2 * m + t // 4)[:, (t % 4) * P:(t % 4 + 1) * P], vt[:, at:at + P], ident)
                last.then_inc(vt_done, 1)

            def attention(layer):
                n0, u0 = plan[f"xq{layer}"]
                q, kk = work[:, 10:12, :], unit(8, 2).rearrange("p (t m) -> p t m", m=N_MEM)
                vh = unit(SSQ)[:, 0:2 * N_MEM].rearrange("p (m d) -> p m d", m=2)
                p, pt = unit(14), unit(15)
                ready = (act_ready, KT * count["act"])
                count["act"] += 1
                stats()
                fresh_pair(n0, u0, ready)
                value_transposes(layer, count["square"])

                def scores(e, h, k):
                    for j in range(4):
                        for d in range(XA_T):
                            tok = e * HALF + j * P
                            last = mm(bank(4, 2)[:, j * N_MEM:(j + 1) * N_MEM], q[:, d, tok:tok + P],
                                      flat(kk[:, ds(XA_T * h + d, 1), :]), start=d == 0, stop=d == 1)
                    if e:
                        xpe.done(last, "S1")
                    else:
                        last.then_inc(first_scores, 1)

                def head(h, more):
                    k = h + XA_H * layer

                    def p_transposes(e):
                        eng.wait_ge(xdve.sem, xdve.at(f"N{e}", k))
                        eng.wait_ge(xdve.sem, xdve.at("O0", k) if e else xdve.at("O1", k - 1))
                        for j in range(4):
                            for m in range(2):
                                at = j * N_MEM + m * P
                                last = tr(bank(6 + m)[:, j * P:(j + 1) * P], p[:, at:at + P], ident)
                        xpe.done(last, f"T{e}")

                    def weighted(e):
                        eng.wait_ge(xact.sem, xact.at(f"P{e}", k))
                        eng.wait_ge(head_ready, k + 1)
                        for d in range(XA_T):
                            for m in range(2):
                                last = mm(bank(6 + d), vh[:, m, d * P:(d + 1) * P], pt[:, m * HALF:(m + 1) * HALF],
                                          start=m == 0, stop=m == 1)
                        xpe.done(last, f"V{e}")

                    def next_q(d):
                        if more:
                            gemm(2 * h + (n0 + 2 + d), n0 + d, 2 * h + (u0 + 2 + d), u0 + d)

                    next_q(0)
                    p_transposes(0)
                    eng.wait_ge(xact.sem, xact.at("E0", k))
                    scores(1, h, k)
                    weighted(0)
                    next_q(1)
                    p_transposes(1)
                    if more:
                        eng.wait_ge(xact.sem, xact.at("E1", k))
                        eng.wait_ge(evac, XA_T * h + (u0 + 2 * XA_T + CREDIT))
                        scores(0, h + 1, k + 1)
                    weighted(1)

                eng.wait_ge(evac, u0 + XA_T + CREDIT)
                eng.wait_ge(v_ready, 4 * (layer + 1))
                scores(0, 0, XA_H * layer)
                link.loop(XA_H - 1, 0, lambda h: head(h, True))
                head(XA_H - 1, False)

            def mlp(layer):
                n0, u0 = plan[f"mlp{layer}"]
                ready = (act_ready, KT * count["act"])
                count["act"] += 1
                per = 2 * MLP_T

                def body(g, first=False):
                    if first:
                        fresh_pair(n0, u0, ready)
                        stats()
                    for b in range(2 if first else 0, MLP_T):
                        gemm(per * g + (n0 + b), n0 + b, U_MLP * g + (u0 + b), u0 + b)
                    n, u = n0 + MLP_T, u0 + MLP_T
                    hidden_pair(per * g + n, n, U_MLP * g + u, u,
                                (hid_ready, MLP_T * g + (MLP_T * MLP_G * layer + CREDIT)))
                    for b in range(1, MLP_T):
                        for o in range(2):
                            n, u = n0 + MLP_T + b, u0 + MLP_T + 2 * b + o
                            gemm(per * g + n, n, U_MLP * g + u, u, kts=MLP_T, first=o * MLP_T * P,
                                 rhs=lambda kt, hl, k: hid[:, kt, hl, k * HALF:(k + 1) * HALF])
                body(0, first=True)
                link.loop(MLP_G - 1, 0, lambda g: body(g + 1))

            def mixer0():
                ua = plan["mix0a"][1]
                project("mix0a", 9, between=stats)
                eng.wait_ge(lruw_in, 32)
                for t in range(LRU_T):
                    eng.wait_ge(lru_conv, t + 1)
                    for k in range(2):
                        u = ua + 9 + 2 * t + k
                        eng.wait_ge(evac, u + 1)
                        w = unit(10)[:, (4 * k + t) * P:(4 * k + t + 1) * P]
                        for half in range(2):
                            at = slice(half * HALF, (half + 1) * HALF)
                            last = mm(slot(u)[:, at], w, unit(t)[:, at], start=True, stop=True)
                        last.then_inc(unit_done, 1)
                for hp in range(2):
                    u = ua + 9 + 2 * LRU_T + hp
                    eng.wait_ge(evac, u + 1)
                    for half in range(2):
                        at = slice(half * HALF, (half + 1) * HALF)
                        last = mm(slot(u)[:, at], small[0:16, hp * P:(hp + 1) * P], unit(11)[0:16, at], start=True,
                                  stop=True)
                    last.then_inc(unit_done, 1)
                project("mix0b", 12, fresh=False)

                def chunk(c, j):
                    e, ks, q = gla["E"][j], gla["KS"][j], gla["QS"][j]
                    eng.wait_ge(gpool.sem, gpool.at("E", c))
                    eng.wait_ge(gexp.sem, gexp.at("stage", c))
                    eng.wait_ge(gev.sem, gev.at("tr", c - 1))
                    transposes(bank(4).rearrange("p (h n) -> p h n", h=4), gla["VS"][j], 4)
                    gpe.done(transposes(bank(5)[:, 0:W2].rearrange("p (h n) -> p h n", h=2), e[:, 7], 2), "tr")
                    for pair in range(4):
                        if pair < 2:
                            eng.wait_ge(gsel.sem, gsel.at(f"L{pair + 2}", c - 1))
                        else:
                            eng.wait_ge(gsel.sem, gsel.at(f"L{pair - 2}", c))
                        for lv in range(2):
                            level = 2 * pair + lv
                            for h in range(GLA_H):
                                par, hp = h % 2, h // 2
                                rows = slice(64 * par, 64 * par + 64)
                                lhs = e[rows, level, hp, :] if level < DIAG else ks[rows, hp, :]
                                rhs = e[rows, level, hp, :] if level < DIAG else q[rows, hp, :]
                                at = lv * W2 + hp * CH
                                last = mm(ps[:, 2 * (pair % 2) + par, at:at + CH], lhs, rhs, start=True, stop=True)
                        gpe.done(last, f"L{pair}")
                    eng.wait_ge(gev.sem, gev.at("tr", c))
                    eng.wait_ge(gsel.sem, gsel.at("S", c - 1))
                    eng.wait_ge(gsel.sem, gsel.at("L3", c))
                    for h in range(GLA_H):
                        par, hp = h % 2, h // 2
                        o = bank(6)[:, h * CH:(h + 1) * CH]
                        mm(o, gla["S"][:, hp, :], gla["QZ"][j][:, h, :], start=True, stop=False)
                        last = mm(o, gla["vtok"][:, h, :], gla["AT"][:, 2 * par + hp, :], start=False, stop=True)
                    gpe.done(last, "o")
                    for h in range(GLA_H):
                        par, hp = h % 2, h // 2
                        last = mm(ps[64 * par:64 * par + 64, 7, hp * P:(hp + 1) * P],
                                  gla["ktok"][:, hp, 64 * par:64 * par + 64], gla["vtok"][:, h, :], start=True,
                                  stop=True)
                    gpe.done(last, "s")

                def body(i):
                    for j in range(2):
                        chunk(2 * i + j, j)
                link.loop(NCH // 2, 0, body)
                eng.wait_ge(gsel.sem, gsel.at("S", NCH - 1))
                for h in range(GLA_H):
                    eng.wait_ge(o_sq, h + 1)
                    if h >= 2:
                        eng.wait_ge(o_ln, h - 1)
                    for half in range(2):
                        at = slice(half * HALF, (half + 1) * HALF)
                        last = mm(bank(4 + 2 * (h % 2), 2)[:, at], ones, unit(4 + h)[:, at], start=True, stop=True)
                    last.then_inc(o_stat, 1)

            def mixer1():
                n0, u0 = plan["mix1"]
                ready = (act_ready, KT * count["act"])
                count["act"] += 1
                fresh_pair(n0, u0, ready)
                stats()
                for k in range(2, 5):
                    gemm(n0 + k, n0 + k, u0 + k, u0 + k)
                eng.wait_ge(evac, u0 + 1 + CREDIT)
                transposes(heads_of(bank(4, 2)), heads(7), NCH).then_inc(ba_t, 1)

                def two(n, u, i=0):
                    for j in range(2):
                        gemm(2 * i + (n + j), n + j, 2 * i + (u + j), u + j)

                link.loop(4, 0, lambda i: two(n0 + 5, u0 + 5, i))
                eng.wait_ge(ba_g, 1)
                mm(bank(6)[:, 0:64], tri, unit(9)[:, 512:576], start=True, stop=True).then_inc(ba_cum, 1)
                link.loop(2 * GDN_H - 6, 0, lambda i: two(n0 + 13, u0 + 13, i))

                def on(steps, name, i):
                    eng.wait_ge(steps.sem, steps.at(name, i))

                def each(first_bank, lhs, rhs, hs=range(GDN_H), start=True, stop=True):
                    for h in hs:
                        last = mm(bank(first_bank + (h // 4 - hs[0] // 4))[:, (h % 4) * P:(h % 4 + 1) * P],
                                  lhs[:, h, :], rhs[:, h, :], start=start, stop=stop)
                    return last

                KN, KNT, R, M, AT, X, Z, Q, S, VN, KD, QG = (heads(t) for t in (7, 8, 9, 10, 11, 12, 13, 14, 15, 16,
                                                                             17, 18))

                def start(p):
                    on(pdve, "dg", p)
                    for k in range(2):
                        last = mm(bank(k), ones, unit(4)[:, k * HALF:(k + 1) * HALF], start=True, stop=True)
                    ppe.done(last, "grow")
                    eng.wait_ge(loaded[1], 16 * p + 16)
                    ppe.done(transposes(heads_of(bank(2, 2)), heads(1), GDN_H), "kt")
                    on(pact, "sqq", p)
                    for k, t in enumerate((7, 14)):
                        for h in range(GDN_H):
                            last = mm(bank(4)[:, 8 * k + h:8 * k + h + 1], heads(t)[:, h, :], ones[:, 0:1], start=True,
                                      stop=True)
                    ppe.done(last, "nrm")

                def state_keys(c):
                    on(fdve, "s", c - 1)
                    on(pdve, f"z{LEVELS - 2}1", c)
                    fpe.done(each(6, KNT, S), "ks")

                def new_values(c):
                    on(fdve, "r", c)
                    fpe.done(each(6, Z, R), "vn")

                def keys_values(p):
                    on(pdve, "kn", p)
                    ppe.done(transposes(heads_of(bank(2, 2)), KN, GDN_H), "knt")
                    eng.wait_ge(loaded[2], 16 * p + 16)
                    on(pact, "rk", p)
                    ppe.done(transposes(heads_of(bank(4, 2)), heads(2), GDN_H), "vt")

                def output_state(c, su_bank=0):
                    on(fact, "vn", c)
                    on(ppool, "kd", c)
                    for h in range(GDN_H):
                        o = bank(6 + h // 4)[:, (h % 4) * P:(h % 4 + 1) * P]
                        mm(o, QG[:, h, :], S[:, h, :], start=True, stop=False)
                        last = mm(o, AT[:, h, :], VN[:, h, :], start=False, stop=True)
                    fpe.done(last, "o")
                    if not su_bank:
                        on(pact, "eg", c + 1)
                    fpe.done(each(su_bank, KD, VN), "su")

                def matrices(p, c):
                    on(pact, "knt", p)
                    if c is not None:
                        on(fdve, "o1", c)
                    ppe.done(each(6, KNT, KNT), "g")
                    on(pdve, "vb", p)
                    ppe.done(each(4, KNT, heads(0)), "qk")
                    on(pdve, "x0", p)
                    ppe.done(transposes(heads_of(bank(0, 2)), X, GDN_H), "z")

                def output_transposes(c, ot_bank=2):
                    on(fdve, "o2", c)
                    fpe.done(transposes(heads_of(bank(ot_bank, 2)), heads(19), GDN_H), "ot")

                def inverse(p, between=None):
                    for n in inv:
                        if n == 2 and between:
                            between()
                        for k in range(2):
                            if n:
                                on(pdve, f"z{n - 1}{k}", p)
                            elif k == 0:
                                on(pact, "z", p)
                            ppe.done(each(k, M, Z, range(4 * k, 4 * k + 4)), f"q{n}{k}")
                        for k in range(2):
                            hs = range(4 * k, 4 * k + 4)
                            on(pact, f"q{n}{k}", p)
                            if n:
                                on(pdve, f"x{n - 1}{k}", p)
                            if n == 0 and k == 0:
                                on(pdve, "at", p)
                            if n < LEVELS - 2:
                                each(4 + k, Q, X, hs)
                            ppe.done(each(6 + k, X, Q, hs), f"x{n}{k}")

                def prepare(p):
                    start(p)
                    keys_values(p)
                    matrices(p, None)
                    inverse(p)

                def both(c, more):
                    state_keys(c)
                    start(c + 1)
                    new_values(c)
                    keys_values(c + 1)
                    output_state(c)
                    matrices(c + 1, c)
                    inverse(c + 1, between=lambda: output_transposes(c))

                def unit_half(j, k):
                    n, u = plan["out1"][0] + j, plan["out1"][1] + j
                    for kt in range(KT):
                        for wp, xp in ((0, 0), (0, 1), (1, 0)):
                            last = mm(slot(u)[:, k * HALF:(k + 1) * HALF], whl[:, n % 2, wp, kt * P:(kt + 1) * P],
                                      act[:, kt, xp, k * HALF:(k + 1) * HALF], start=kt == wp == xp == 0,
                                      stop=kt == KT - 1 and wp == 1)
                    return last

                def finish(c):
                    state_keys(c)
                    eng.wait_ge(w_split, plan["out1"][0] + 2 + CREDIT)
                    eng.wait_ge(fdve.sem, fdve.at("lo", NCH // 2 - 1))
                    unit_half(0, 0)
                    new_values(c)
                    output_state(c, su_bank=4)
                    unit_half(1, 0)
                    output_transposes(c, ot_bank=4)
                    eng.wait_ge(fdve.sem, fdve.at("lo", NCH - 1))
                    for j in range(2):
                        unit_half(j, 1).then_inc(unit_done, 1)

                gdn_chunks(link, prepare, finish, both, 0)

            eng.sem_inc(unit_done, CREDIT)
            for s in (xpe, gpe, ppe, fpe):
                s.credit(eng)
            eng.wait_ge(const_in, 32)
            mixer0()
            for layer in range(2):
                if layer:
                    stats()
                    mixer1()
                project(f"out{layer}", KT, fresh=not layer, between=mem_stat_, after_units=3 if layer else 2)
                stats()
                eng.wait_ge(mem_ready, layer + 1)
                project(f"kv{layer}", 2 * KT, fresh=False, width=N_MEM,
                        rhs=lambda kt, hl, k: memhl[:, hl, kt * N_MEM:(kt + 1) * N_MEM])
                attention(layer)
                project(f"xo{layer}", KT)
                stats()
                mlp(layer)
            stats()


def host_arrays(x):
    import numpy as np

    def block(w):
        full = np.zeros((D, P), w.dtype)
        full[:, :w.shape[1]] = w
        return full.reshape(KT, P, P).transpose(1, 0, 2).reshape(P, D)

    def blocks(w):
        return [block(w[:, n:n + P]) for n in range(0, w.shape[1], P)]

    def vector(v):
        return v.reshape(-1, P).T

    w_in, stream = x["ab_w_in"][0], []
    q, k, v, g, lr, lx, lg = np.split(w_in, [256, 512, 1024, 1536, 1552, 2064], axis=1)
    stream += blocks(lx) + blocks(lg) + blocks(lr) + blocks(v) + blocks(g) + blocks(q) + blocks(k)
    out0 = x["ab_w_out"][0]
    outs = [np.concatenate([out0[512:], out0[:512]]), x["gdn_w_out"][0]]
    for layer in range(2):
        if layer:
            w = x["gdn_w_in"][0]
            stream += blocks(w[:, 4 * GDN_H * P:])
            for h in range(GDN_H):
                for kind in range(4):
                    at = kind * GDN_H * P + h * P
                    stream += blocks(w[:, at:at + P])
        stream += blocks(outs[layer]) + blocks(x["xa_w_kv"][layer]) + blocks(x["xa_w_q"][layer])
        stream += blocks(x["xa_w_o"][layer])
        w1, w2 = x["mlp_w1"][layer], x["mlp_w2"][layer]
        for g in range(MLP_G):
            rows = slice(g * MLP_T * P, (g + 1) * MLP_T * P)
            stream += blocks(w1[:, rows])
            part = w2[rows].reshape(MLP_T, P, KT // 2, 2, P).transpose(2, 1, 3, 0, 4)
            stream += list(part.reshape(KT // 2, P, D))
    conv0 = x["lru_conv_w"][0].reshape(4, LRU_T, P).transpose(2, 1, 0).reshape(P, 16)
    conv1 = x["gdn_conv_w"][0].reshape(4, 24, P).transpose(2, 1, 0).reshape(P, 96)
    vectors = {"lru_conv_w": conv0, "gdn_conv_w": conv1,
               "gdn_dt_bias": np.repeat(x["gdn_dt_bias"], P, 0), "gdn_a_log": np.repeat(x["gdn_a_log"], P, 0)}
    pvec = np.concatenate([vectors[name] if name in vectors else vector(x[name]) for name, _ in VECTORS], axis=1)
    lru_w = np.stack([x["lru_w_a"][0], x["lru_w_x"][0]]).transpose(2, 0, 1, 3).reshape(P, D)
    tok = np.arange(P)
    consts = np.concatenate([np.eye(P), np.ones((P, P)), tok[:, None] <= tok[None, :]], axis=1).astype(np.float32)
    levels = []
    for level in range(LEVELS):
        half = P >> (level + 1)
        low, up, blk = tok // half % 2 == 0, tok // half % 2 == 1, tok // (2 * half)
        levels.append(low[:, None] & up[None, :] & (blk[:, None] == blk[None, :]))
    masks = np.stack(levels + [np.eye(P, dtype=bool)] + [m.T for m in levels] + [tok[:, None] <= tok[None, :]], axis=1)

    def tiles(a):
        return a.T.reshape(KT, P, -1).transpose(1, 0, 2)

    return {"xT": tiles(x["x"][0]), "memT": tiles(x["mem"][0]).reshape(P, KT * N_MEM), "wstream": np.stack(stream),
            "lru_w": lru_w, "gk_w2": x["gla_gk_w2"][0], "pvec_in": pvec, "consts_in": consts,
            "masks_in": masks.astype(np.float32)}


def kernel(**inputs):
    import numpy as np
    import concourse.bacc as bacc
    from concourse.bass_utils import run_bass_kernel_spmd as run

    nc = bacc.Bacc("TRN2", target_bir_lowering=False, num_devices=1)
    arrays = {k: np.ascontiguousarray(a) for k, a in host_arrays({k: np.asarray(v) for k, v in inputs.items()}).items()}
    args = {k: nc.dram_tensor(f"{k}_dram", a.shape, mybir.dt.from_np(a.dtype), kind="ExternalInput").ap()
            for k, a in arrays.items()}
    outT = nc.dram_tensor("outT_dram", (P, KT, SEQ), F32, kind="ExternalOutput").ap()
    build(nc, outT=outT, **args)
    r = run(nc, [{f"{k}_dram": a for k, a in arrays.items()}], core_ids=[0])
    got = r.results[0]["outT_dram"]
    return got.transpose(1, 0, 2).reshape(D, SEQ).T.reshape(1, SEQ, D)
```
